# Optimizing a Trainium2 kernel written in Bass

```python
import jax, jax.numpy as jnp
from jax import lax
import numpy as np

D_MODEL = 1024
BATCH = 1
SEQ = 256
DEPTH = 2
DEC_BATCH = 8
DEC_SEQ = 1
PAST_LEN = 1024
PAGE_SIZE = 128

N_POOL_LAYERS = (DEPTH + 1) // 2
N_NSA_LAYERS = DEPTH // 2

POOL_WINDOWS = (2, 4, 8, 16)
N_POOL_GROUPS = len(POOL_WINDOWS)
POOL_GROUP = D_MODEL // N_POOL_GROUPS
POOL_BUF = max(POOL_WINDOWS) - 1

N_HEADS = 16
HEAD_DIM = D_MODEL // N_HEADS
N_KV_HEADS = 4
GQA = N_HEADS // N_KV_HEADS
CMP_BLOCK = 32
SLC_BLOCK = 64
SLC_TOPK = 16
WINDOW = 512
Q_BLOCK = 64
N_BRANCH = 3
KV_W = N_KV_HEADS * HEAD_DIM
Q_W = N_HEADS * HEAD_DIM
NSA_IN_COLS = Q_W + 6 * KV_W + N_BRANCH * N_HEADS
FORCE_BONUS = 1000.0

D_FF = 3584
N_EXPERTS = 8
TOP_K = 2

EPS = 1e-6
NEG = -1e30

kernel_name = 'pool_nsa_hybrid_decode_step'

def rmsnorm(x, g):
    xf = x.astype(jnp.float32)
    y = xf * lax.rsqrt(jnp.mean(xf * xf, axis=-1, keepdims=True) + EPS)
    return (y * g.astype(jnp.float32)).astype(x.dtype)

def alibi_slopes():
    h = jnp.arange(1, N_HEADS + 1, dtype=jnp.float32)
    return jnp.exp2(-8.0 * h / N_HEADS).reshape(N_KV_HEADS, GQA)

def masked_softmax(s, mask, axes):
    s = jnp.where(mask, s, NEG)
    m = jnp.max(s, axis=axes, keepdims=True)
    p = jnp.where(mask, jnp.exp(s - m), 0.0)
    return p / jnp.maximum(jnp.sum(p, axis=axes, keepdims=True), 1e-30)

def pool_mix(h, buf, w_pool, pool_scale):
    B, Q, D = h.shape
    P = buf.shape[1]
    full = jnp.concatenate([buf, h], axis=1)
    c = jnp.pad(jnp.cumsum(full.astype(jnp.float32), axis=1), ((0, 0), (1, 0), (0, 0)))
    end = P + 1 + jnp.arange(Q)
    c_end = c[:, end]
    parts = []
    for g, w in enumerate(POOL_WINDOWS):
        sl = slice(g * POOL_GROUP, (g + 1) * POOL_GROUP)
        start = jnp.maximum(end - w, 0)
        cnt = (end - start).astype(jnp.float32)[None, :, None]
        parts.append((c_end[..., sl] - c[:, start, sl]) / cnt)
    pooled = (jnp.concatenate(parts, axis=-1) - h.astype(jnp.float32)).astype(h.dtype)
    mixed = jnp.einsum('bqgc,gce->bqge', pooled.reshape(B, Q, N_POOL_GROUPS, POOL_GROUP), w_pool)
    y = mixed.reshape(B, Q, D) * pool_scale
    return y, full[:, -POOL_BUF:]

def nsa_project(h, w_in):
    B, L, _ = h.shape
    z = h @ w_in
    q = z[..., :Q_W].reshape(B, L, N_KV_HEADS, GQA, HEAD_DIM)
    kv = z[..., Q_W:Q_W + 6 * KV_W].reshape(B, L, 6, N_KV_HEADS, HEAD_DIM)
    gates = jax.nn.sigmoid(z[..., Q_W + 6 * KV_W:].astype(jnp.float32)).reshape(B, L, N_BRANCH, N_KV_HEADS, GQA)
    return q, kv, gates

def compress(x, w_cmp):
    B, L = x.shape[:2]
    nc = L // CMP_BLOCK
    xb = x[:, :nc * CMP_BLOCK].reshape(B, nc, CMP_BLOCK, N_KV_HEADS, HEAD_DIM)
    return jnp.einsum('bnckd,ck->bnkd', xb, w_cmp)

def to_slc_blocks(x):
    B, L = x.shape[:2]
    ns = -(-L // SLC_BLOCK)
    x = jnp.pad(x, ((0, 0), (0, ns * SLC_BLOCK - L), (0, 0), (0, 0)))
    return x.reshape(B, ns, SLC_BLOCK, N_KV_HEADS, HEAD_DIM).transpose(0, 3, 1, 2, 4)

def nsa_attend(q, gates, q_pos, kc, vc, ks, vs, kw, vw, w_pos):
    f32 = jnp.float32
    scale = HEAD_DIM ** -0.5
    slopes = alibi_slopes()
    tq = q_pos.astype(f32)
    B, Q = q.shape[:2]

    nc = kc.shape[1]
    c_idx = jnp.arange(nc)
    c_end = (c_idx + 1) * CMP_BLOCK - 1
    c_mid = c_idx.astype(f32) * CMP_BLOCK + (CMP_BLOCK - 1) / 2
    s_c = jnp.einsum('bqkgd,bckd->bkgqc', q, kc, preferred_element_type=f32) * scale \
        - slopes[:, :, None, None] * (tq[:, None] - c_mid[None, :])
    p_c = masked_softmax(s_c, c_end[None, :] <= q_pos[:, None], -1)
    o_c = jnp.einsum('bkgqc,bckd->bqkgd', p_c, vc)

    ns = ks.shape[2]
    r = SLC_BLOCK // CMP_BLOCK
    imp = jnp.pad(p_c.sum(axis=2), ((0, 0), (0, 0), (0, 0), (0, ns * r - nc)))
    imp = imp.reshape(B, N_KV_HEADS, Q, ns, r).sum(-1)
    blk = q_pos // SLC_BLOCK
    j = jnp.arange(ns)[None, :]
    valid = j <= blk[:, None]
    forced = (j == 0) | (j == blk[:, None]) | (j == blk[:, None] - 1)
    score = jnp.where(valid, imp + jnp.where(forced, FORCE_BONUS, 0.0), -1.0)
    _, idx = lax.top_k(score, min(SLC_TOPK, ns))

    gather = jax.vmap(jax.vmap(lambda blocks, ids: blocks[ids]))
    gk = gather(ks, idx)
    gv = gather(vs, idx)
    pos = idx[..., None] * SLC_BLOCK + jnp.arange(SLC_BLOCK)
    dist = (tq[:, None, None] - pos.astype(f32))[:, :, None]
    s_s = jnp.einsum('bqkgd,bkqnsd->bkgqns', q, gk, preferred_element_type=f32) * scale \
        - slopes[:, :, None, None, None] * dist
    mask_s = (pos <= q_pos[:, None, None])[:, :, None]
    p_s = masked_softmax(s_s, mask_s, (-2, -1))
    o_s = jnp.einsum('bkgqns,bkqnsd->bqkgd', p_s, gv)

    wp = w_pos[None, :]
    tp = q_pos[:, None]
    s_w = jnp.einsum('bqkgd,bwkd->bkgqw', q, kw, preferred_element_type=f32) * scale \
        - slopes[:, :, None, None] * (tq[:, None] - w_pos.astype(f32)[None, :])
    mask_w = (wp <= tp) & (tp - wp < WINDOW) & (wp >= 0)
    p_w = masked_softmax(s_w, mask_w, -1)
    o_w = jnp.einsum('bkgqw,bwkd->bqkgd', p_w, vw)

    o = gates[:, :, 0, :, :, None] * o_c + gates[:, :, 1, :, :, None] * o_s + gates[:, :, 2, :, :, None] * o_w
    return o.astype(q.dtype)

def nsa_prompt(h, w_in, w_cmp_k, w_cmp_v, w_o):
    B, L, _ = h.shape
    q, kv, gates = nsa_project(h, w_in)
    kc = compress(kv[:, :, 0], w_cmp_k)
    vc = compress(kv[:, :, 1], w_cmp_v)
    ks = to_slc_blocks(kv[:, :, 2])
    vs = to_slc_blocks(kv[:, :, 3])
    kwp = jnp.pad(kv[:, :, 4:6], ((0, 0), (WINDOW, 0), (0, 0), (0, 0), (0, 0)))
    nqb = L // Q_BLOCK
    qb = q.reshape(B, nqb, Q_BLOCK, N_KV_HEADS, GQA, HEAD_DIM).transpose(1, 0, 2, 3, 4, 5)
    gb = gates.reshape(B, nqb, Q_BLOCK, N_BRANCH, N_KV_HEADS, GQA).transpose(1, 0, 2, 3, 4, 5)

    def one_block(args):
        qi, gi, i = args
        t0 = i * Q_BLOCK
        q_pos = t0 + jnp.arange(Q_BLOCK)
        band = lax.dynamic_slice_in_dim(kwp, t0, WINDOW + Q_BLOCK, axis=1)
        w_pos = t0 - WINDOW + jnp.arange(WINDOW + Q_BLOCK)
        return nsa_attend(qi, gi, q_pos, kc, vc, ks, vs, band[:, :, 0], band[:, :, 1], w_pos)

    o = lax.map(one_block, (qb, gb, jnp.arange(nqb)))
    o = o.transpose(1, 0, 2, 3, 4, 5).reshape(B, L, Q_W)
    wb = min(WINDOW, L)
    return o @ w_o, kv[:, :, :4], kv[:, L - wb:, 4:6]

def nsa_sample(h, past, win_buf, w_in, w_cmp_k, w_cmp_v, w_o):
    B, Q, _ = h.shape
    q, kv, gates = nsa_project(h, w_in)
    P = past.shape[1]
    full = jnp.concatenate([past, kv[:, :, :4]], axis=1)
    kc = compress(full[:, :, 0], w_cmp_k)
    vc = compress(full[:, :, 1], w_cmp_v)
    ks = to_slc_blocks(full[:, :, 2])
    vs = to_slc_blocks(full[:, :, 3])
    wb = win_buf.shape[1]
    win = jnp.concatenate([win_buf, kv[:, :, 4:6]], axis=1)
    w_pos = P - wb + jnp.arange(wb + Q)
    q_pos = P + jnp.arange(Q)
    o = nsa_attend(q, gates, q_pos, kc, vc, ks, vs, win[:, :, 0], win[:, :, 1], w_pos)
    keep = min(WINDOW, wb + Q)
    return o.reshape(B, Q, Q_W) @ w_o, kv[:, :, :4], win[:, wb + Q - keep:]

def swiglu(h, wg, wu, wd):
    return (jax.nn.silu(h @ wg) * (h @ wu)) @ wd

def moe(h, w_router, wg, wu, wd):
    logits = (h @ w_router).astype(jnp.float32)
    top_v, top_i = lax.top_k(logits, TOP_K)
    wts = jax.nn.softmax(top_v, axis=-1)
    gate = jnp.sum(jax.nn.one_hot(top_i, N_EXPERTS, dtype=jnp.float32) * wts[..., None], axis=-2)
    acc = jnp.zeros(h.shape, jnp.float32)
    for e in range(N_EXPERTS):
        acc = acc + gate[..., e, None] * swiglu(h, wg[e], wu[e], wd[e])
    return acc.astype(h.dtype)

def setup_inputs(seed: int = 0) -> dict:
    key = jax.random.key(seed)
    k = jax.random.split(key, 24)
    f32 = jnp.float32
    n_pages = PAST_LEN // PAGE_SIZE
    n_used = DEC_BATCH * n_pages
    n_phys = n_used + n_used // 4
    win_buf = min(WINDOW, PAST_LEN)

    def nrm(kk, shape, s):
        return jax.random.normal(kk, shape, f32) * s

    page_table = jax.random.permutation(k[5], n_phys)[:n_used].astype(jnp.int32).reshape(DEC_BATCH, n_pages)
    return {
        'x_prompt': nrm(k[0], (BATCH, SEQ, D_MODEL), 1.0),
        'x_sample': nrm(k[1], (DEC_BATCH, DEC_SEQ, D_MODEL), 1.0),
        'state_pool': nrm(k[2], (N_POOL_LAYERS, DEC_BATCH, POOL_BUF, D_MODEL), 1.0),
        'cache_kv': nrm(k[3], (N_NSA_LAYERS, n_phys, PAGE_SIZE, 4, N_KV_HEADS, HEAD_DIM), 1.0),
        'state_win': nrm(k[4], (N_NSA_LAYERS, DEC_BATCH, win_buf, 2, N_KV_HEADS, HEAD_DIM), 1.0),
        'page_table': page_table,
        'norm_mix': 1.0 + nrm(k[6], (DEPTH, D_MODEL), 0.05),
        'w_pool': nrm(k[7], (N_POOL_LAYERS, N_POOL_GROUPS, POOL_GROUP, POOL_GROUP), POOL_GROUP ** -0.5),
        'pool_scale': 0.5 + nrm(k[8], (N_POOL_LAYERS, D_MODEL), 0.05),
        'w_nsa_in': nrm(k[9], (N_NSA_LAYERS, D_MODEL, NSA_IN_COLS), D_MODEL ** -0.5),
        'w_cmp_k': (1.0 + nrm(k[10], (N_NSA_LAYERS, CMP_BLOCK, N_KV_HEADS), 0.1)) / CMP_BLOCK,
        'w_cmp_v': (1.0 + nrm(k[11], (N_NSA_LAYERS, CMP_BLOCK, N_KV_HEADS), 0.1)) / CMP_BLOCK,
        'w_nsa_out': nrm(k[12], (N_NSA_LAYERS, Q_W, D_MODEL), Q_W ** -0.5),
        'norm_ffn': 1.0 + nrm(k[13], (DEPTH, D_MODEL), 0.05),
        'w_ffn_gate': nrm(k[14], (N_POOL_LAYERS, D_MODEL, D_FF), D_MODEL ** -0.5),
        'w_ffn_up': nrm(k[15], (N_POOL_LAYERS, D_MODEL, D_FF), D_MODEL ** -0.5),
        'w_ffn_down': nrm(k[16], (N_POOL_LAYERS, D_FF, D_MODEL), D_FF ** -0.5),
        'w_router': nrm(k[17], (N_NSA_LAYERS, D_MODEL, N_EXPERTS), D_MODEL ** -0.5),
        'w_moe_gate': nrm(k[18], (N_NSA_LAYERS, N_EXPERTS, D_MODEL, D_FF), D_MODEL ** -0.5),
        'w_moe_up': nrm(k[19], (N_NSA_LAYERS, N_EXPERTS, D_MODEL, D_FF), D_MODEL ** -0.5),
        'w_moe_down': nrm(k[20], (N_NSA_LAYERS, N_EXPERTS, D_FF, D_MODEL), D_FF ** -0.5),
        'norm_final': 1.0 + nrm(k[21], (D_MODEL,), 0.05),
    }

def reference(x_prompt, x_sample, state_pool, cache_kv, state_win, page_table,
              norm_mix, w_pool, pool_scale, w_nsa_in, w_cmp_k, w_cmp_v, w_nsa_out,
              norm_ffn, w_ffn_gate, w_ffn_up, w_ffn_down,
              w_router, w_moe_gate, w_moe_up, w_moe_down, norm_final):
    xp, xs = x_prompt, x_sample
    pool_p, pool_s, kv_p, kv_s, win_p, win_s = [], [], [], [], [], []
    for i in range(DEPTH):
        j = i // 2
        hp = rmsnorm(xp, norm_mix[i])
        hs = rmsnorm(xs, norm_mix[i])
        if i % 2 == 0:
            yp, sp = pool_mix(hp, hp[:, :0], w_pool[j], pool_scale[j])
            ys, ss = pool_mix(hs, state_pool[j], w_pool[j], pool_scale[j])
            pool_p.append(sp)
            pool_s.append(ss)
        else:
            yp, kp, wp = nsa_prompt(hp, w_nsa_in[j], w_cmp_k[j], w_cmp_v[j], w_nsa_out[j])
            past = cache_kv[j, page_table]
            past = past.reshape(page_table.shape[0], -1, 4, N_KV_HEADS, HEAD_DIM)
            ys, ksn, wsn = nsa_sample(hs, past, state_win[j], w_nsa_in[j], w_cmp_k[j], w_cmp_v[j], w_nsa_out[j])
            kv_p.append(kp)
            kv_s.append(ksn)
            win_p.append(wp)
            win_s.append(wsn)
        xp = xp + yp
        xs = xs + ys
        hp = rmsnorm(xp, norm_ffn[i])
        hs = rmsnorm(xs, norm_ffn[i])
        if i % 2 == 0:
            xp = xp + swiglu(hp, w_ffn_gate[j], w_ffn_up[j], w_ffn_down[j])
            xs = xs + swiglu(hs, w_ffn_gate[j], w_ffn_up[j], w_ffn_down[j])
        else:
            xp = xp + moe(hp, w_router[j], w_moe_gate[j], w_moe_up[j], w_moe_down[j])
            xs = xs + moe(hs, w_router[j], w_moe_gate[j], w_moe_up[j], w_moe_down[j])
    y_prompt = rmsnorm(xp, norm_final)
    y_sample = rmsnorm(xs, norm_final)
    return (y_prompt, y_sample, jnp.stack(pool_p), jnp.stack(pool_s), jnp.stack(kv_p), jnp.stack(kv_s), jnp.stack(win_p), jnp.stack(win_s))


_drawn_inputs = setup_inputs


def setup_inputs(seed=0):
    import zlib

    import numpy as np

    out = dict(_drawn_inputs(seed))
    spreads = {}
    factors = {'w_cmp_k': 8.0, 'w_cmp_v': 6.163}
    for name, (base, spread) in spreads.items():
        noise = np.random.default_rng([zlib.crc32(name.encode()), seed]).standard_normal(out[name].shape)
        drawn = base * np.exp(spread * noise) if base else spread * noise
        out[name] = __import__('jax').numpy.asarray(drawn.astype(out[name].dtype))
    for name, factor in factors.items():
        out[name] = (out[name] * factor).astype(out[name].dtype)
    return out
```

```python
from contextlib import ExitStack

import numpy as np

import concourse.bass as bass
from concourse import mybir

F32 = mybir.dt.float32
I32 = mybir.dt.int32
ALU = mybir.AluOpType
ACT = mybir.ActivationFunctionType
AX = mybir.AxisListType.X

P = 128
D = 1024
NC = D // P
TP = 256
TS = 8
T = TP + TS
EPS = 1e-6
NEG = -1e30
POOL_WINDOWS = (2, 4, 8, 16)
POOL_BUF = 15
NH, NKV, GQA, HD = 16, 4, 4, 64
KVW = NKV * HD
QW = NH * HD
PAST = 1024
PAGE = 128
NPAGE = PAST // PAGE
CMP = 32
NCMP_P = TP // CMP
NCMP_D = PAST // CMP
SLC = 64
NSLC_D = PAST // SLC
WIN = 512
FORCE = 1000.0
SCALE = HD ** -0.5
DFF = 3584
NE = 8
FG = 512
NG = DFF // FG
FS = FG // P
NSLOT = 7
TILE = NC * FG
CAP = T // 3
NTC = 3
MAXI = NE + 8
EXPERT_TILES = 3 * NG
USES_BEFORE = 4
SLOPES = np.exp2(-8.0 * np.arange(1, NH + 1, dtype=np.float32) / NH).astype(np.float32)


def constants():
    p = np.arange(P)
    f = np.float32
    out = {}
    out["ident"] = np.eye(P)
    out["ones"] = np.ones((P, P))
    t = np.arange(TP)[None, :]
    out["dist_p"] = np.where(t <= P + p[:, None], t - (P + p[:, None]), NEG)
    out["dist_d"] = np.broadcast_to(np.arange(PAST) - PAST, (P, PAST))
    mid = np.arange(NCMP_D) * CMP + (CMP - 1) / 2
    out["dist_c"] = np.broadcast_to(mid - PAST, (P, NCMP_D))
    out["slope"] = SLOPES[p % NH][:, None]
    i, n = np.arange(2)[None, :, None, None], np.arange(NCMP_P)[None, None, None, :]
    tq = i * P + p[:, None, None, None]
    ok = (n + 1) * CMP - 1 <= tq
    sl = SLOPES[None, None, :, None]
    out["cmp_bias"] = np.where(ok, -sl * (tq - (n * CMP + (CMP - 1) / 2)), NEG + 0 * sl).reshape(P, -1)
    out["cmp_mask"] = ok.reshape(P, -1)
    kp, g, k2 = np.arange(2)[:, None, None], np.arange(4)[None, :, None], np.arange(2)[None, None, :]
    out["head_of"] = (p[:, None, None, None] // NCMP_P == (2 * kp + k2) * GQA + g).reshape(P, -1)
    out["blk_of"] = (p[None, :] % NCMP_P == p[:, None])
    out["inv_cnt"] = np.broadcast_to(1.0 / (np.arange(15) + 1), (P, 15))
    out["same_kv"] = p[:, None] // GQA == p[None, :] // GQA
    forced = np.zeros(NSLC_D)
    forced[[0, NSLC_D - 1]] = FORCE
    out["forced"] = np.broadcast_to(forced, (P, NSLC_D))
    out["order"] = np.broadcast_to(np.arange(NSLC_D) + 1, (P, NSLC_D))
    out["is_head"] = p[:, None] % NH == np.arange(NH)[None, :]
    out["spread_b"] = p[:, None] == p[None, :] // NH
    out["is_b"] = p[:, None] // NH == np.arange(TS)[None, :]
    out["iota_s"] = np.broadcast_to(np.arange(CAP), (P, CAP))
    out["before"] = p[:, None] < np.arange(CAP)[None, :]
    out["e_order"] = np.broadcast_to(NE - np.arange(NE), (P, NE))
    out["k_rows"] = (p[:, None, None] == (2 * np.arange(2)[None, :, None] + p[None, None, :] // HD)).reshape(P, -1)
    out["quarter"] = p[:, None] // CMP == np.arange(4)[None, :]
    out["over_code"] = np.broadcast_to(np.arange(NE, 3 * NE), (P, 2 * NE))
    out["over_min"] = np.broadcast_to(np.repeat([CAP, 2 * CAP], NE), (P, 2 * NE))
    out["items0"] = np.broadcast_to(np.arange(MAXI + 1) * (np.arange(MAXI + 1) < NE), (P, MAXI + 1))
    return {k: np.asarray(v, dtype=f) for k, v in out.items()}


def const_columns():
    at, cols = 0, {}
    for name, a in constants().items():
        cols[name] = (at, a.shape[1])
        at += a.shape[1]
    return cols, at


class Steps:

    def __init__(self, eng, sem):
        self.eng, self.sem, self.n, self.per, self.it = eng, sem, 0, 0, None

    def __call__(self, ins):
        ins.then_inc(self.sem, 1)
        self.n += 1

    def settle(self):
        if self.it is None:
            self.eng.wait_ge(self.sem, self.n)
        else:
            self.eng.wait_ge(self.sem, self.it * self.per + self.n)

    def loop(self, it, per):
        self.it, self.per, self.start = it, per, self.n

    def end(self):
        assert self.n - self.start == self.per, (self.n - self.start, self.per)
        self.it = None


def bc(ap, axis, n):
    shape = list(ap.shape)
    shape.insert(axis, n)
    return ap.unsqueeze(axis).to_broadcast(shape)


def build(nc, x_prompt, x_sample, state_pool, cache_kv, state_win, page_table, norm_mix, w_pool, pool_scale,
          w_nsa_in, w_cmp_k, w_cmp_v, w_nsa_out, norm_ffn, w_ffn_gate, w_ffn_up, w_ffn_down, w_router,
          w_moe_gate, w_moe_up, w_moe_down, norm_final, consts,
          y_prompt, y_sample, new_pool_prompt, new_pool_sample, new_kv_prompt, new_kv_sample, new_win_prompt,
          new_win_sample):
    ctx = ExitStack()
    with ctx:
        def sb(name, shape, dt=F32):
            return ctx.enter_context(nc.sbuf_tensor(name, shape, dt))

        def sem(name):
            return ctx.enter_context(nc.semaphore(name))

        mm = nc.tensor.matmul
        tr = nc.tensor.transpose

        Q_SLOT0 = (EXPERT_TILES + 3) % NSLOT

        cols, n_const = const_columns()
        cst = sb("cst", [P, n_const])

        def K(name, rows=P):
            a, n = cols[name]
            return cst[0:rows, a:a + n]

        ident = K("ident")
        ones = K("ones")
        ring = sb("ring", [P, NSLOT, TILE])
        xT = sb("xT", [P, NC, T])
        hT = sb("hT", [P, NC, T])
        vec_rows = sb("vec_rows", [48, P])
        vecT = sb("vecT", [P, 6, NC])
        V_MIX0, V_MIX1, V_FFN0, V_FFN1, V_FINAL, V_POOL = range(6)
        router = sb("router", [P, NC, NE])
        w_gates = sb("w_gates", [P, NC, 48])
        rms = sb("rms", [P, T])
        rstd = sb("rstd", [P, T])
        pages = sb("pages", [1, TS * NPAGE], I32)
        wn = sb("wn", [P, 2, NKV])
        wcT = sb("wcT", [NKV, 2, CMP])
        wkT = sb("wkT", [P, 2, 2, CMP])
        wb = sb("wb", [P, 2, NKV, 4])
        AR = 15800
        arena = sb("arena", [P, AR])
        banks = ctx.enter_context(nc.psum_tensor("banks", [P, 8, 512], F32))

        def carve(base, *sizes):
            out, at = [], 0
            for n in sizes:
                out.append(base[:, at:at + n])
                at += n
            assert at <= base.shape[1], (at, base.shape)
            return out

        early = ring[:, 5:7, :].rearrange("p s n -> p (s n)")
        x_nat_f, xs_nat, st_nat, wpool_f, stT_f = carve(early, 2 * D, D, D, 2 * D, NC * TS * POOL_BUF)
        x_nat = x_nat_f.rearrange("p (j d) -> p j d", j=2)
        wpool = wpool_f.rearrange("p (g c e) -> p g c e", g=4, c=2)
        stT = stT_f.rearrange("p (c b j) -> p c b j", c=NC, b=TS)
        sq_f, s2_f, s4_f, s8_f, s16_f, pl_f, pool_out, edge_f, ssum_f = carve(
            arena[:, :], NC * T, 8 * TP, 6 * TP, 4 * TP, 2 * TP, NC * T, D, 30, 16)
        sq = sq_f.rearrange("p (c t) -> p c t", c=NC)
        s2, s4, s8, s16 = (a.rearrange("p (c t) -> p c t", t=TP) for a in (s2_f, s4_f, s8_f, s16_f))
        pl = pl_f.rearrange("p (c t) -> p c t", c=NC)
        ssum = ssum_f.rearrange("p (c b) -> p c b", c=2)
        _, hid_f, sg_f = carve(arena[:, :], NC * T, 2 * FS * T, 2 * T)
        hid = hid_f.rearrange("p (s f t) -> p s f t", s=2, f=FS)
        sg = sg_f.rearrange("p (s t) -> p s t", s=2)
        (zkv_f, qT_f, qz_f, kvn_f, kvs, sc_s, sc_w, sc_c, gn_f, pcp_f, kcp_f, vcp_f, vcz_f, pcT, sm,
         sm16, gd_f, gdec, pn_f, pst, spread) = carve(
            arena[:, :], 12 * T, 8 * T, 2048, 3072, 1536, PAST + 1, WIN + 1, NCMP_D, 3 * 48, 256, 16, 16,
            1024, 256, 16, 64, 48, 3, 2 * TS, 16, 64)
        wq = [arena[:, 20 * T + 2048:20 * T + 2048 + TILE], ring[:, Q_SLOT0, :]]
        gz = rms
        vcn_p = sc_w[:, 0:KVW]
        zkv = zkv_f.rearrange("p (c t) -> p c t", c=12)
        KC_, VC_, KS_, VS_, KW_, VW_ = range(6)
        qT = qT_f.rearrange("p (a g t) -> p a g t", a=2, g=GQA)
        qz = qz_f.rearrange("p (a b m) -> p a b m", a=2, b=TS)
        kvn = kvn_f.rearrange("p (j n) -> p j n", j=2)
        gn = gn_f.rearrange("p (j n) -> p j n", j=3)
        pcp = pcp_f.rearrange("p (i h n) -> p i h n", i=2, h=NH)
        kcp = kcp_f.rearrange("p (a n) -> p a n", a=2)
        vcp = vcp_f.rearrange("p (a n) -> p a n", a=2)
        vcz = vcz_f.rearrange("p (m n) -> p m n", m=8)
        gd = gd_f.rearrange("p (r h) -> p r h", r=3)
        pn = pn_f.rearrange("p (r b) -> p r b", r=2)
        late = ring[:, 0:3, :].rearrange("p s n -> p (s n)")
        kb0, kb1, kb2, kt_f, kw_f, vcT_f, kcT_f = carve(late, 3072, 3072, 3072, 1024, 1024, 512, 128)
        kbuf = [kb0, kb1, kb2]
        KT = kt_f.rearrange("p (s t) -> p s t", s=2)
        KWn = kw_f.rearrange("p (c n) -> p c n", c=4)
        vcT = vcT_f.rearrange("p (b a n) -> p b a n", b=TS, a=2)
        kcT = kcT_f.rearrange("p (s a n) -> p s a n", s=2, a=2)
        PR = kt_f.rearrange("p (s r t) -> p s r t", s=2, r=2)
        PT = kw_f.rearrange("p (s t) -> p s t", s=2)
        vcn = late[:, 9216:9216 + 2048].rearrange("p (b n) -> p b n", b=TS)
        PsT_f, PwT_f, PcT, PnT_f = carve(qz_f, 1024, 512, 128, 256)
        PsT = PsT_f.rearrange("p (c m) -> p c m", c=8)
        PwT = PwT_f.rearrange("p (c m) -> p c m", c=4)
        PnT = PnT_f.rearrange("p (r m) -> p r m", r=2)
        (_, xn_f, xe_f, mh_f, msg, ysb_f, ynat, Pm_f, Gm_f, GT, lg_f, l2_f, eq_f, oh1_f, oh2_f, sel_f, gate_f,
         posx_f, gx_f, one, ovr, items_f, yout_f) = carve(
            arena[:, :], NC * T, NTC * D, NC * CAP, 2 * FS * CAP, FS * CAP, NC * CAP, D, T, T, T, 24, 24, 24, 24, 24,
            24, 24, 72, 72, 24, 64, 24, 3 * D)
        xn = xn_f.rearrange("p (j d) -> p j d", j=NTC)
        xe = xe_f.rearrange("p (c s) -> p c s", c=NC)
        mh = mh_f.rearrange("p (b f s) -> p b f s", b=2, f=FS)
        ysb = ysb_f.rearrange("p (c s) -> p c s", c=NC)
        Pm, Gm = (a.rearrange("p (j s) -> p j s", j=NTC) for a in (Pm_f, Gm_f))
        lg, l2, eq, oh1, oh2, sel, gate = (a.rearrange("p (j e) -> p j e", j=NTC)
                                           for a in (lg_f, l2_f, eq_f, oh1_f, oh2_f, sel_f, gate_f))
        posx, gx = (a.rearrange("p (j r e) -> p j r e", j=NTC, r=3) for a in (posx_f, gx_f))
        posc, gxc = (a.rearrange("p (j c) -> p j c", j=NTC) for a in (posx_f, gx_f))
        yout = yout_f.rearrange("p (j d) -> p j d", j=3)
        items = sb("items", [1, MAXI + 1], I32)
        n_items = sb("n_items", [1, 1], I32)
        eps = sb("eps", [P, 1])

        consts_in, vecs_in, xin, xsin, states_in, wpool_in, router_in, wgates_in, wcmp_in, pages_in = (
            sem(n) for n in ("consts_in", "vecs_in", "xin", "xsin", "states_in", "wpool_in", "router_in", "wgates_in",
                             "wcmp_in", "pages_in"))
        tile_in = [sem(f"tile_in{s}") for s in range(NSLOT)]
        kb_in = [sem(f"kb_in{i}") for i in range(3)]
        stored, rows_moved, kw_in = sem("stored"), sem("rows_moved"), sem("kw_in")
        xt_ps, xt_act, xt_dve, st_ps, st_sb, vec_ps, vec_sb, wkT_ps, wkT_sb, wb_ready = (
            sem(n) for n in ("xt_ps", "xt_act", "xt_dve", "st_ps", "st_sb", "vec_ps", "vec_sb", "wkT_ps", "wkT_sb",
                             "wb_ready"))
        sq_ready, ms_ready, rms_ready, h_ready = (sem(n) for n in ("sq_ready", "ms_ready", "rms_ready", "h_ready"))
        po_ps, po_sb, pooled, mixed, pool_added = (sem(n) for n in ("po_ps", "po_sb", "pooled", "mixed", "pool_added"))
        gu_ps, silu_done, hid_done, down_ps, ffn_added = (sem(n) for n in (
            "gu_ps", "silu_done", "hid_done", "down_ps", "ffn_added"))
        proj_ps, proj_act, proj_dve, nat_ps, nat_act, nat_dve, gates_ps, gate_e, gates_ready = (sem(n) for n in (
            "proj_ps", "proj_act", "proj_dve", "nat_ps", "nat_act", "nat_dve", "gates_ps", "gate_e", "gates_ready"))
        qz_zero, qz_ready, cp_ready, vcp_ps, vcp_sb, rep_ps, vcz_ready, cs_ps, cs_in, cs_exp, cs_w, pcT_ps, pcT_sb = (
            sem(n) for n in ("qz_zero", "qz_ready", "cp_ready", "vcp_ps", "vcp_sb", "rep_ps", "vcz_ready", "cs_ps",
                             "cs_in", "cs_exp", "cs_w", "pcT_ps", "pcT_sb"))
        kt_ps, kt_act, kt_dve, sc_done, comp_ps, kc_sb, kc_used = (sem(n) for n in (
            "kt_ps", "kt_act", "kt_dve", "sc_done", "comp_ps", "kc_sb", "kc_used"))
        dec_read, dec_max, dec_exp, imp_in, imp_ps, gd_ps, dprob = (sem(n) for n in (
            "dec_read", "dec_max", "dec_exp", "imp_in", "imp_ps", "gd_ps", "dprob"))
        ps_ps, ps_in, ps_max, ps_exp, pw_ready, pt_ps, pt_sb, pv_done, o_sb = (sem(n) for n in (
            "ps_ps", "ps_in", "ps_max", "ps_exp", "pw_ready", "pt_ps", "pt_sb", "pv_done", "o_sb"))
        vcn_ps, vcn_sb, pdt_ps, pdt_sb, od_ps, od_sb, wo_ps, wo_added = (sem(n) for n in (
            "vcn_ps", "vcn_sb", "pdt_ps", "pdt_sb", "od_ps", "od_sb", "wo_ps", "wo_added"))
        xn_ps, xn_act, xn_dve, lg_ps, top_gap, top_exp, sel_ready, pos_ps, table_ready = (sem(n) for n in (
            "xn_ps", "xn_act", "xn_dve", "lg_ps", "top_gap", "top_exp", "sel_ready", "pos_ps", "table_ready"))
        P_ready, G_ready, xe_ps, xe_sb, mgu_ps, msilu, mhid, mdn_ps = (sem(n) for n in (
            "P_ready", "G_ready", "xe_ps", "xe_sb", "mgu_ps", "msilu", "mhid", "mdn_ps"))
        ysb_done, gt_ps, gt_sb, yn_ps, yn_sb, so_ps, so_added, yt_ps, yt_sb = (sem(n) for n in (
            "ysb_done", "gt_ps", "gt_sb", "yn_ps", "yn_sb", "so_ps", "so_added", "yt_ps", "yt_sb"))
        dve_steps, eps_ready, wq_ready = sem("dve_steps"), sem("eps_ready"), sem("wq_ready")

        KV_TILE0 = EXPERT_TILES
        Q_TILE0 = KV_TILE0 + 3
        O_TILE0 = Q_TILE0 + 2
        assert O_TILE0 + 2 == USES_BEFORE * NSLOT
        N_PROJ = 21
        UNITS = 6 * TS

        def slot_view(s, shape):
            if shape == "up":
                return ring[:, s, :].rearrange("p (c f) -> p c f", c=NC)
            return ring[:, s, :].rearrange("p (q n) -> p q n", q=FS)

        def extra(s):
            return 16 if s in (O_TILE0 % NSLOT, (O_TILE0 + 1) % NSLOT) else 0

        def wait_tile(eng, t):
            eng.wait_ge(tile_in[t % NSLOT], 16 * (t // NSLOT + 1) + (16 if t >= O_TILE0 else 0))

        def wait_expert_tile(eng, i, j):
            s, u = j % NSLOT, j // NSLOT
            eng.wait_ge(tile_in[s], i * (16 * 3) + (16 * (USES_BEFORE + u + 1) + extra(s)))

        def ffn_tile(wg, wu, wd, j):
            g, kind = divmod(j, 3)
            if kind < 2:
                w = (wg, wu)[kind]
                return w.rearrange("(c p) f -> p c f", p=P)[:, :, g * FG:(g + 1) * FG], "up"
            return wd.rearrange("(q p) n -> p q n", p=P)[:, g * FS:(g + 1) * FS, :], "down"

        def kb_value(n):
            return sum(16 * (4 if m < 2 * TS else 9) for m in range(n % 3, n + 1, 3))

        GCOL = QW + 6 * KVW
        w_in_v = w_nsa_in[0].rearrange("(c p) n -> p c n", p=P)
        block = ctx.enter_context(nc.Block())

        @block.sync
        def _(sp):
            sp.dma_start(x_nat, x_prompt[0].rearrange("(j p) d -> p j d", p=P)).then_inc(xin, 16)
            sp.dma_start(xs_nat[0:TS, :], x_sample.rearrange("b q d -> (b q) d")).then_inc(xsin, 16)
            sp.dma_start(cst[:, :], consts).then_inc(consts_in, 16)
            for n, v in enumerate((norm_mix[0], norm_mix[1], norm_ffn[0], norm_ffn[1], norm_final, pool_scale[0])):
                sp.dma_start(vec_rows[8 * n:8 * n + 8, :], v.rearrange("(c p) -> c p", p=P)).then_inc(vecs_in, 16)
            sp.dma_start(st_nat[0:TS * POOL_BUF, :], state_pool[0].rearrange("b j d -> (b j) d")).then_inc(states_in, 16)
            for g in range(4):
                sp.dma_start(wpool[:, g], w_pool[0, g].rearrange("(c p) e -> p c e", p=P)).then_inc(wpool_in, 16)

            for t in range(EXPERT_TILES + 5):
                if t < NSLOT:
                    if t == 5:
                        sp.wait_ge(mixed, NC)
                else:
                    g, kind = divmod(t - NSLOT, 3)
                    if kind < 2:
                        sp.wait_ge(gu_ps, FS * (g + 1))
                    else:
                        sp.wait_ge(down_ps, NC * (g + 1))
                s = t % NSLOT
                if t < EXPERT_TILES:
                    src, shape = ffn_tile(w_ffn_gate[0], w_ffn_up[0], w_ffn_down[0], t)
                elif t < Q_TILE0:
                    c0 = QW + (t - KV_TILE0) * FG
                    src, shape = w_in_v[:, :, c0:c0 + FG], "up"
                else:
                    c0 = (t - Q_TILE0) * FG
                    src, shape = w_in_v[:, :, c0:c0 + FG], "up"
                sp.dma_start(slot_view(s, shape), src).then_inc(tile_in[s], 16)
                if t == 4:
                    sp.dma_start(router[:, :, :], w_router[0].rearrange("(c p) e -> p c e", p=P)).then_inc(router_in, 16)
                    sp.dma_start(w_gates[:, :, :], w_in_v[:, :, GCOL:GCOL + 48]).then_inc(wgates_in, 16)
                    sp.dma_start(pages[0:1, :], page_table.rearrange("(o b) p -> o (b p)", o=1)).then_inc(pages_in, 16)
                if t == 8:
                    sp.dma_start(new_win_sample[0, :, 0:WIN - 1].rearrange("b w s k d -> b (w s k d)"),
                                 state_win[0, :, 1:WIN].rearrange("b w s k d -> b (w s k d)")).then_inc(rows_moved, 16)
            for n in range(2):
                t = O_TILE0 + n
                g, kind = divmod(t - NSLOT, 3)
                sp.wait_ge(down_ps if kind == 2 else gu_ps, (NC if kind == 2 else FS) * (g + 1))
                for k2 in range(2):
                    r0 = (2 * n + k2) * GQA * HD
                    sp.dma_start(slot_view(t % NSLOT, "down")[HD * k2:HD * (k2 + 1)],
                                 w_nsa_out[0, r0:r0 + GQA * HD].rearrange("(g d) n -> d g n", d=HD)
                                 ).then_inc(tile_in[t % NSLOT], 16)

            sp.wait_ge(proj_ps, 12)
            sp.wait_ge(pages_in, 16)

            def load_pages(b, half, dst, c0, c1, done):
                for n in range(4):
                    at = b * NPAGE + half * 4 + n
                    pid = sp.value_load(pages[0:1, at:at + 1], min_val=0, max_val=cache_kv.shape[1] - 1)
                    src = cache_kv[0, bass.ds(pid, 1)].rearrange("o t s k d -> (o t) (s k d)")
                    sp.dma_start(dst[:, n], src[:, c0:c1]).then_inc(done, 16)

            def expert_tile(i, j, weights):
                s = j % NSLOT
                if j >= NSLOT or not isinstance(i, int):
                    g, kind = divmod(j - NSLOT if j >= NSLOT else j + 2 * NSLOT, 3)
                    back = 0 if j >= NSLOT else NG
                    sp.wait_ge(mgu_ps if kind < 2 else mdn_ps, i * NG + (g + 1 - back))
                src, shape = ffn_tile(*weights, j)
                sp.dma_start(slot_view(s, shape), src).then_inc(tile_in[s], 16)

            first = [w[0, 0] for w in (w_moe_gate, w_moe_up, w_moe_down)]
            for b in range(TS):
                for half in range(2):
                    n = 2 * b + half
                    if n >= 3:
                        sp.wait_ge(comp_ps, n - 2)
                    load_pages(b, half, kbuf[n % 3].rearrange("p (n c) -> p n c", n=4), 0, 3 * KVW, kb_in[n % 3])
                if b:
                    sp.wait_ge(kt_ps, 6 * b)
                sp.dma_start(KWn, state_win[0, b, :, 0].rearrange("(c p) k d -> p c (k d)", p=P)).then_inc(kw_in, 16)
                if b in (2, 4):
                    if b == 2:
                        sp.wait_ge(proj_ps, N_PROJ - 1)
                    expert_tile(0, 3 + (b == 4), first)
            for b in range(TS):
                n = 2 * TS + b
                if b < 3:
                    sp.wait_ge(comp_ps, n - 2)
                else:
                    sp.wait_ge(od_ps, b - 2)
                for half in range(2):
                    load_pages(b, half, kbuf[n % 3][:, half * 1024:(half + 1) * 1024].rearrange("p (n c) -> p n c", n=4),
                               3 * KVW, 4 * KVW, kb_in[n % 3])
                sp.dma_start(kbuf[n % 3][:, 2048:3072].rearrange("p (c n) -> p c n", c=4),
                             state_win[0, b, :, 1].rearrange("(c p) k d -> p c (k d)", p=P)).then_inc(kb_in[n % 3], 16)
            sp.wait_ge(od_ps, TS)
            for j in range(3):
                expert_tile(0, j, first)
            sp.wait_ge(wo_ps, NC)
            for j in range(5, EXPERT_TILES):
                expert_tile(0, j, first)

            def dyn(w, e):
                return w[0, bass.ds(e, 1)].rearrange("o a b -> (o a) b")

            with sp.Fori(1, NE) as i:
                for j in range(EXPERT_TILES):
                    expert_tile(i, j, [dyn(w, i) for w in (w_moe_gate, w_moe_up, w_moe_down)])
            sp.wait_ge(table_ready, 1)
            count = sp.value_load(n_items[0:1, 0:1], min_val=NE, max_val=MAXI)
            with sp.If(count > NE):
                with sp.Fori(NE, count) as i:
                    code = sp.value_load(items[0:1, bass.ds(i, 1)], min_val=0, max_val=3 * NE - 1)
                    e = sp.snap(code % NE, min_val=0, max_val=NE - 1)
                    for j in range(EXPERT_TILES):
                        expert_tile(i, j, [dyn(w, e) for w in (w_moe_gate, w_moe_up, w_moe_down)])
            sp.wait_ge(rows_moved, 16)
            sp.wait_ge(stored, 16 * 11)

        @block.gpsimd
        def _(gp):
            for s, w in enumerate((w_cmp_k, w_cmp_v)):
                for q in range(4):
                    gp.dma_start(wn[CMP * q:CMP * (q + 1), s, :], w[0]).then_inc(wcmp_in, 16)
            with nc.allow_non_contiguous_dma(reason="256 numbers"):
                for s, w in enumerate((w_cmp_k, w_cmp_v)):
                    gp.dma_start(wcT[:, s, :], w[0].rearrange("c k -> k c")).then_inc(wcmp_in, 16)
            gp.dma_start(new_pool_sample[0, :, 0:POOL_BUF - 1], state_pool[0, :, 1:POOL_BUF]).then_inc(stored, 16)
            gp.wait_ge(po_sb, 2)
            gp.dma_start(new_pool_prompt[0, 0], pool_out[0:POOL_BUF, :]).then_inc(stored, 16)
            gp.dma_start(new_pool_sample[0, :, POOL_BUF - 1], pool_out[POOL_BUF:POOL_BUF + TS, :]).then_inc(stored, 16)
            gp.wait_ge(mixed, NC)
            gp.wait_ge(stored, 16 * 3)
            gp.memset(qz_f, 0.0).then_inc(qz_zero, 1)
            gp.wait_ge(nat_act, 5)
            gp.wait_ge(nat_dve, 4)
            for j in range(2):
                rows = slice(j * P, (j + 1) * P)
                gp.dma_start(new_kv_prompt[0, 0, rows].rearrange("t s k d -> t (s k d)"), kvn[:, j, 0:4 * KVW]
                             ).then_inc(stored, 16)
                gp.dma_start(new_win_prompt[0, 0, rows].rearrange("t s k d -> t (s k d)"), kvn[:, j, 4 * KVW:]
                             ).then_inc(stored, 16)
            gp.dma_start(new_kv_sample[0].rearrange("b q s k d -> (b q) (s k d)"), kvs[0:TS, 0:4 * KVW]
                         ).then_inc(stored, 16)
            gp.dma_start(new_win_sample[0, :, WIN - 1].rearrange("b s k d -> b (s k d)"), kvs[0:TS, 4 * KVW:]
                         ).then_inc(stored, 16)
            gp.wait_ge(yt_sb, 6)
            gp.dma_start(y_prompt[0].rearrange("(j p) d -> p j d", p=P), yout[:, 0:2, :]).then_inc(stored, 16)
            gp.dma_start(y_sample.rearrange("b q d -> (b q) d"), yout[0:TS, 2, :]).then_inc(stored, 16)

        @block.tensor
        def _(pe):
            def norm_sums(k):
                for half in range(2):
                    pe.wait_ge(sq_ready, 2 * k + half + 1)
                    for c in range(4 * half, 4 * half + 4):
                        last = mm(banks[:, 7, 0:T], ones, sq[:, c], start=(c == 0), stop=(c == NC - 1))
                last.then_inc(ms_ready, 1)

            def h_chunk(k, c):
                pe.wait_ge(h_ready, NC * k + c + 1)

            pe.wait_ge(consts_in, 16)
            pe.wait_ge(xin, 16)
            pe.wait_ge(xsin, 16)
            for c in range(NC):
                for j in range(2):
                    tr(banks[:, c, j * P:(j + 1) * P], x_nat[:, j, c * P:(c + 1) * P], ident)
                tr(banks[:, c, TP:T], xs_nat[0:TS, c * P:(c + 1) * P], ident[0:TS, 0:TS]).then_inc(xt_ps, 1)
            pe.wait_ge(vecs_in, 6 * 16)
            pe.wait_ge(xt_dve, 3)
            tr(banks[:, 2, 0:48], vec_rows[:, :], ident[0:48, 0:48]).then_inc(vec_ps, 1)
            pe.wait_ge(xt_act, 4)
            norm_sums(0)
            pe.wait_ge(wcmp_in, 10 * 16)
            for a in range(2):
                last = mm(banks[:, 4, 64 * a:64 * (a + 1)], K("k_rows", NKV)[:, P * a:P * (a + 1)],
                          wcT[:, :, :].rearrange("k s c -> k (s c)"), start=True, stop=True)
            last.then_inc(wkT_ps, 1)
            n_state = TS * POOL_BUF
            pe.wait_ge(states_in, 16)
            for c in range(NC):
                last = tr(banks[:, c // 4, (c % 4) * n_state:(c % 4 + 1) * n_state],
                          st_nat[0:n_state, c * P:(c + 1) * P], ident[0:n_state, 0:n_state])
                if c % 4 == 3:
                    last.then_inc(st_ps, 1)
            pe.wait_ge(xt_dve, 4)
            for c in range(NC):
                h_chunk(0, c)
                last = tr(banks[0:POOL_BUF + TS, 5 + c // 4, (c % 4) * P:(c % 4 + 1) * P],
                          hT[:, c, TP - POOL_BUF:T], ident)
                if c % 4 == 3:
                    last.then_inc(po_ps, 1)
            pe.wait_ge(wpool_in, 4 * 16)
            pe.wait_ge(st_sb, 2)
            pe.wait_ge(vec_sb, 1)
            pe.wait_ge(wkT_sb, 1)
            pe.wait_ge(po_sb, 2)
            for g in range(4):
                pe.wait_ge(pooled, g + 1)
                for e in range(2):
                    for c in range(2):
                        last = mm(banks[:, 2 * g + e, 0:T], wpool[:, g, c, e * P:(e + 1) * P], pl[:, 2 * g + c],
                                  start=(c == 0), stop=(c == 1))
                    last.then_inc(mixed, 1)
            norm_sums(1)

            def dense_up(g):
                for s in range(FS):
                    u = FS * g + s
                    if u >= 2:
                        pe.wait_ge(hid_done, u - 1)
                    for kind in range(2):
                        t = 3 * g + kind
                        if s == 0:
                            wait_tile(pe, t)
                        w = slot_view(t % NSLOT, "up")
                        for c in range(NC):
                            if u == 0 and kind == 0:
                                h_chunk(1, c)
                            last = mm(banks[:, 2 * kind + u % 2, 0:T], w[:, c, s * P:(s + 1) * P], hT[:, c],
                                      start=(c == 0), stop=(c == NC - 1))
                    last.then_inc(gu_ps, 1)

            def dense_down(g):
                t = 3 * g + 2
                wait_tile(pe, t)
                pe.wait_ge(hid_done, FS * (g + 1))
                w = slot_view(t % NSLOT, "down")
                for d in range(NC):
                    u = NC * g + d
                    if u >= 4:
                        pe.wait_ge(ffn_added, u - 3)
                    for s in range(FS):
                        last = mm(banks[:, 4 + u % 4, 0:T], w[:, s, d * P:(d + 1) * P], hid[:, g % 2, s],
                                  start=(s == 0), stop=(s == FS - 1))
                    last.then_inc(down_ps, 1)

            for g in range(NG + 1):
                if g < NG:
                    dense_up(g)
                if g:
                    dense_down(g - 1)
            norm_sums(2)

            for n in range(N_PROJ):
                if n >= 4:
                    pe.wait_ge(proj_dve if n % 2 else proj_act, (n - 4) // 2 + 1)
                if n in (12, 16):
                    pe.wait_ge(wq_ready, 2 * ((n - 12) // 4 + 1))
                if n == N_PROJ - 1:
                    pe.wait_ge(wgates_in, 16)
                    w, rows = w_gates[:, :, :], 48
                else:
                    t = KV_TILE0 + n // 4
                    if n % 4 == 0 and n < 12:
                        wait_tile(pe, t)
                    w, rows = slot_view(t % NSLOT, "up"), P
                for c in range(NC):
                    if n == 0:
                        h_chunk(2, c)
                    if n == N_PROJ - 1:
                        lhs = w[:, c, :]
                    elif n < 12:
                        lhs = w[:, c, (n % 4) * P:(n % 4 + 1) * P]
                    else:
                        at = c * FG + (n - 12) % GQA * P
                        lhs = wq[(n - 12) // GQA][:, at:at + P]
                    last = mm(banks[0:rows, n % 4, 0:T], lhs, hT[:, c], start=(c == 0), stop=(c == NC - 1))
                last.then_inc(proj_ps, 1)
            pe.wait_ge(proj_act, 6)
            pe.wait_ge(proj_dve, 6)
            for w in range(9):
                j, quad = divmod(w, 3)
                rows = P if j < 2 else TS
                if w >= 4:
                    pe.wait_ge(nat_dve if w % 2 else nat_act, (w - 4) // 2 + 1)
                for c in range(4):
                    last = tr(banks[0:rows, 4 + w % 4, c * P:(c + 1) * P], zkv[:, 4 * quad + c, j * P:j * P + rows],
                              ident)
                last.then_inc(nat_ps, 1)
            pe.wait_ge(proj_act, 11)
            pe.wait_ge(nat_dve, 3)
            for j in range(3):
                rows = P if j < 2 else TS
                last = tr(banks[0:rows, 5, 48 * j:48 * (j + 1)], gz[0:48, j * P:j * P + rows], ident[0:48, 0:48])
            last.then_inc(gates_ps, 1)
            pe.wait_ge(cp_ready, 2)
            pe.wait_ge(nat_dve, 4)
            for a in range(2):
                last = tr(banks[0:NCMP_P, 7, P * a:P * (a + 1)], vcp[:, a, :], ident)
            last.then_inc(vcp_ps, 1)
            pe.wait_ge(vcp_sb, 1)
            pe.wait_ge(proj_dve, 10)
            pe.wait_ge(nat_act, 4)
            for h in range(NH):
                k, g = divmod(h, GQA)
                a, k2 = divmod(k, 2)
                half = slice(HD * k2, HD * (k2 + 1))
                for i in range(2):
                    at = 256 + (i * NH + h) * NCMP_P
                    last = mm(banks[:, 7 - k2, at:at + NCMP_P], qT[half, a, g, i * P:(i + 1) * P], kcp[half, a, :],
                              start=True, stop=True)
            last.then_inc(cs_ps, 1)
            pe.wait_ge(proj_act, 10)
            mm(banks[:, 2, 0:KVW], K("blk_of", NCMP_P), vcn_p[0:NCMP_P, :], start=True, stop=True).then_inc(rep_ps, 1)

            pe.wait_ge(qz_ready, 1)
            pe.wait_ge(wb_ready, 1)
            pe.wait_ge(nat_act, 5)
            pe.wait_ge(cs_in, 1)
            pe.wait_ge(gate_e, 1)
            for r, kind in enumerate((KS_, KW_)):
                for b in range(TS):
                    for a in range(2):
                        mm(banks[:, 3, r:r + 1], qz[:, a, b], zkv[:, 2 * kind + a, TP + b:TP + b + 1],
                           start=(r == 0 and b == 0 and a == 0), stop=(b == TS - 1 and a == 1), skip_group_check=True)

            def key_unit(n):
                b, u = divmod(n, 6)
                if u < 4:
                    hf, a = divmod(u, 2)
                    m = 2 * b + hf
                    if a == 0:
                        pe.wait_ge(kb_in[m % 3], 64 * (m // 3 + 1))
                    src = kbuf[m % 3].rearrange("p (n c) -> p n c", n=4)[:, :, 2 * KVW + P * a:2 * KVW + P * (a + 1)]
                else:
                    a = u - 4
                    if a == 0:
                        pe.wait_ge(kw_in, 16 * (b + 1))
                    src = KWn[:, :, P * a:P * (a + 1)]
                if n >= 2:
                    pe.wait_ge(kt_dve if n % 2 else kt_act, (n - 2) // 2 + 1)
                for c in range(4):
                    last = tr(banks[:, 4 + n % 2, c * P:(c + 1) * P], src[:, c, :], ident)
                last.then_inc(kt_ps, 1)

            def unit_scores(n):
                b, u = divmod(n, 6)
                a, bank = (u % 2, u // 2) if u < 4 else (u - 4, 2)
                pe.wait_ge(kt_dve if n % 2 else kt_act, n // 2 + 1)
                if n == 4:
                    pe.wait_ge(vcz_ready, 2)
                mm(banks[:, bank, :], qz[:, a, b], KT[:, n % 2], start=(b == 0 and a == 0),
                   stop=(b == TS - 1 and a == 1), skip_group_check=True).then_inc(sc_done, 1)

            def compress_half(m):
                b, hf = divmod(m, 2)
                if hf == 0 and b >= 2:
                    pe.wait_ge(kc_sb, b - 1)
                v = kbuf[m % 3].rearrange("p (n c) -> p n c", n=4)
                for s in range(2):
                    for pg in range(4):
                        for a in range(2):
                            at = ((s * NPAGE + 4 * hf + pg) * 2 + a) * 8
                            last = mm(banks[:, 6 + b % 2, at:at + 8], v[:, pg, s * KVW + P * a:s * KVW + P * (a + 1)],
                                      wb[:, s, 2 * a:2 * a + 2, :], start=True, stop=True)
                last.then_inc(comp_ps, 1)

            def compressed_scores(b):
                pe.wait_ge(kc_sb, b + 1)
                for a in range(2):
                    last = mm(banks[:, 3, 32:32 + NCMP_D], qz[:, a, b], kcT[:, b % 2, a],
                              start=False, stop=(b == TS - 1 and a == 1), skip_group_check=True)
                last.then_inc(kc_used, 1)

            for n in range(UNITS):
                key_unit(n)
                if n:
                    unit_scores(n - 1)
                if n % 6 in (1, 3):
                    compress_half(2 * (n // 6) + (n % 6) // 2)
                if n % 6 == 0 and n:
                    compressed_scores(n // 6 - 1)
            unit_scores(UNITS - 1)
            compressed_scores(TS - 1)

            pe.wait_ge(cs_w, 1)
            pe.wait_ge(kc_sb, TS)
            for i in range(2):
                last = tr(banks[:, 7, P * i:P * (i + 1)], pcp_f[:, P * i:P * (i + 1)], ident)
            last.then_inc(pcT_ps, 1)

            pe.wait_ge(gates_ready, 1)
            mm(banks[:, 6, 64:112], K("spread_b", TS), gn[0:TS, 2, :], start=True, stop=True).then_inc(gd_ps, 1)
            pe.wait_ge(imp_in, 1)
            mm(banks[:, 6, 0:NSLC_D], K("same_kv"), sm16[:, 0:NSLC_D], start=True, stop=True).then_inc(imp_ps, 1)
            def where(n):
                m, r = divmod(n, 4)
                a, g = divmod(m, GQA)
                k2, i = divmod(r, 2)
                return m, a, g, k2, i, slice(HD * k2, HD * (k2 + 1))

            def prompt_scores(n):
                m, a, g, k2, i, half = where(n)
                if n >= 2:
                    pe.wait_ge(ps_in, n - 1)
                for r, kind in enumerate((KS_, KW_)):
                    last = mm(banks[:, 4 + n % 2, 256 * r:256 * r + P * (i + 1)], qT[half, a, g, i * P:(i + 1) * P],
                              zkv[half, 2 * kind + a, 0:P * (i + 1)], start=True, stop=True)
                last.then_inc(ps_ps, 1)

            def prompt_transposes(n):
                i = n % 2
                pe.wait_ge(pw_ready, n + 1)
                if n >= 2:
                    pe.wait_ge(pt_sb, n - 1)
                for r in range(2):
                    for t in range(i + 1):
                        at = (r * (i + 1) + t) * P
                        last = tr(banks[:, 2 + n % 2, at:at + P], PR[:, n % 2, r, t * P:(t + 1) * P], ident)
                last.then_inc(pt_ps, 1)

            def prompt_values(n):
                m, a, g, k2, i, half = where(n)
                if n % 4 == 0:
                    if m >= 2:
                        pe.wait_ge(o_sb, m - 1)
                    mm(banks[:, m % 2, 0:TP], vcz[:, m], pcT, start=True, stop=False, skip_group_check=True)
                pe.wait_ge(pt_sb, n + 1)
                for r, kind in enumerate((VS_, VW_)):
                    for t in range(i + 1):
                        at = (r * (i + 1) + t) * P
                        c0 = kind * KVW + (2 * a + k2) * HD
                        last = mm(banks[half, m % 2, i * P:(i + 1) * P], kvn[:, t, c0:c0 + HD],
                                  PT[:, n % 2, at:at + P], start=False, stop=(r == 1 and t == i),
                                  skip_group_check=True)
                last.then_inc(pv_done, 1)

            pe.wait_ge(dec_read, 1)
            pe.wait_ge(pcT_sb, 1)
            for n in range(34):
                if n < 32:
                    prompt_scores(n)
                if 1 <= n < 33:
                    prompt_transposes(n - 1)
                if n >= 2:
                    prompt_values(n - 2)

            pe.wait_ge(o_sb, 8)
            pe.wait_ge(pt_sb, 32)
            for b in range(TS):
                for a in range(2):
                    n = 2 * b + a
                    last = tr(banks[0:NCMP_D, n // 4, (n % 4) * P:(n % 4 + 1) * P], vcT[:, b, a], ident)
                if b % 2:
                    last.then_inc(vcn_ps, 1)
            pe.wait_ge(dprob, 1)
            for c in range(8):
                last = tr(banks[:, 4 + c // 4, (c % 4) * P:(c % 4 + 1) * P], sc_s[:, c * P:(c + 1) * P], ident)
                if c % 4 == 3:
                    last.then_inc(pdt_ps, 1)
            for c in range(4):
                last = tr(banks[:, 6, c * P:(c + 1) * P], sc_w[:, c * P:(c + 1) * P], ident)
            last.then_inc(pdt_ps, 1)
            tr(banks[0:NCMP_D, 7, 0:P], sc_c, ident)
            for r in range(2):
                last = tr(banks[0:TS, 7, P * (r + 1):P * (r + 2)], pn[:, r, :], ident)
            last.then_inc(pdt_ps, 1)
            pe.wait_ge(pdt_sb, 5)
            pe.wait_ge(vcn_sb, 4)
            for r, kind in enumerate((VS_, VW_)):
                for a in range(2):
                    mm(banks[:, 2, P * a:P * (a + 1)], kvs[0:TS, kind * KVW + P * a:kind * KVW + P * (a + 1)],
                       PnT[0:TS, r, :], start=(r == 0 and a == 0), stop=False, skip_group_check=True)
            for b in range(TS):
                n = 2 * TS + b
                pe.wait_ge(kb_in[n % 3], kb_value(n))
                hs = slice(NH * b, NH * (b + 1))
                for a in range(2):
                    out = banks[:, 2, P * a + NH * b:P * a + NH * (b + 1)]
                    mm(out, vcn[0:NCMP_D, b, P * a:P * (a + 1)], PcT[0:NCMP_D, hs], start=False, stop=False,
                       skip_group_check=True)
                    for c in range(12):
                        src = kbuf[n % 3][:, c * KVW + P * a:c * KVW + P * (a + 1)]
                        prob = PsT[:, c, hs] if c < 8 else PwT[:, c - 8, hs]
                        last = mm(out, src, prob, start=False, stop=(c == 11), skip_group_check=True)
                last.then_inc(od_ps, 1)

            for c in range(2):
                wait_tile(pe, O_TILE0 + c)
            pe.wait_ge(od_sb, 1)
            for c in range(NC):
                if c >= 4:
                    pe.wait_ge(wo_added, c - 3)
                for m in range(8):
                    a, g = divmod(m, GQA)
                    last = mm(banks[:, 4 + c % 4, 0:T],
                              slot_view((O_TILE0 + a) % NSLOT, "down")[:, g, c * P:(c + 1) * P], hT[:, m],
                              start=(m == 0), stop=(m == 7))
                last.then_inc(wo_ps, 1)
            norm_sums(3)

            for c in range(NC):
                h_chunk(3, c)
            pe.wait_ge(router_in, 16)
            for j in range(NTC):
                for c in range(NC):
                    last = mm(banks[0:CAP, 6, NE * j:NE * (j + 1)], hT[:, c, j * CAP:(j + 1) * CAP], router[:, c, :],
                              start=(c == 0), stop=(c == NC - 1))
            last.then_inc(lg_ps, 1)
            for w in range(6):
                j, hf = divmod(w, 2)
                for c in range(4):
                    last = tr(banks[0:CAP, w, c * P:(c + 1) * P], hT[:, 4 * hf + c, j * CAP:(j + 1) * CAP], ident)
                last.then_inc(xn_ps, 1)
            pe.wait_ge(sel_ready, 1)
            for j in range(NTC):
                for q in range(j + 1):
                    mm(banks[0:CAP, 6, 32 + NE * j:32 + NE * (j + 1)],
                       K("before", CAP) if q == j else ones[0:CAP, 0:CAP], sel[0:CAP, q], start=(q == 0), stop=(q == j))
            for q in range(NTC):
                last = mm(banks[:, 6, 64:64 + NE], ones[0:CAP, :], sel[0:CAP, q], start=(q == 0), stop=(q == NTC - 1))
            last.then_inc(pos_ps, 1)

            def gather():
                for c in range(NC):
                    for j in range(NTC):
                        last = mm(banks[:, 6 + c // 4, (c % 4) * CAP:(c % 4 + 1) * CAP],
                                  xn[0:CAP, j, c * P:(c + 1) * P], Pm[0:CAP, j, :], start=(j == 0), stop=(j == NTC - 1))
                last.then_inc(xe_ps, 1)

            pe.wait_ge(xn_act, 3)
            pe.wait_ge(xn_dve, 3)
            pe.wait_ge(table_ready, 1)
            count = pe.value_load(n_items[0:1, 0:1], min_val=NE, max_val=MAXI)
            pe.wait_ge(P_ready, 1)
            gather()

            def expert_up(i, g):
                if g == 0:
                    pe.wait_ge(xe_sb, i * 2 + 2)
                if g == 1:
                    pe.wait_ge(so_added, i * NC + NC)
                if g >= 2:
                    pe.wait_ge(mhid, i * NG + (g - 1))
                for kind in range(2):
                    wait_expert_tile(pe, i, 3 * g + kind)
                    w = slot_view((3 * g + kind) % NSLOT, "up")
                    for s in range(FS):
                        for c in range(NC):
                            last = mm(banks[:, 2 * kind + g % 2, s * CAP:(s + 1) * CAP], w[:, c, s * P:(s + 1) * P],
                                      xe[:, c], start=(c == 0), stop=(c == NC - 1))
                last.then_inc(mgu_ps, 1)

            def expert_down(i, g):
                wait_expert_tile(pe, i, 3 * g + 2)
                pe.wait_ge(mhid, i * NG + (g + 1))
                w = slot_view((3 * g + 2) % NSLOT, "down")
                for d in range(NC):
                    for s in range(FS):
                        last = mm(banks[:, 4 + d // 4, (d % 4) * CAP:(d % 4 + 1) * CAP], w[:, s, d * P:(d + 1) * P],
                                  mh[:, g % 2, s], start=(g == 0 and s == 0 and d % 4 == 0),
                                  stop=(g == NG - 1 and s == FS - 1), skip_group_check=True)
                last.then_inc(mdn_ps, 1)

            OUT_BANKS = (6, 7, 1, 3)
            with pe.Fori(0, count) as i:
                for g in range(NG):
                    expert_up(i, g)
                    if g:
                        expert_down(i, g - 1)
                expert_down(i, NG - 1)
                pe.wait_ge(P_ready, i + 2)
                gather()
                pe.wait_ge(G_ready, i + 1)
                for j in range(NTC):
                    last = tr(banks[0:CAP, 1, j * CAP:(j + 1) * CAP], Gm[0:CAP, j, :], ident[0:CAP, 0:CAP])
                last.then_inc(gt_ps, 1)
                for hf in range(2):
                    pe.wait_ge(ysb_done, i * 2 + (hf + 1))
                    for c in range(4):
                        last = tr(banks[0:CAP, 2 + hf, c * P:(c + 1) * P], ysb[:, 4 * hf + c, :], ident)
                    last.then_inc(yn_ps, 1)
                pe.wait_ge(gt_sb, i + 1)
                pe.wait_ge(yn_sb, i * 2 + 2)
                pe.wait_ge(xe_sb, i * 2 + 4)
                for c in range(NC):
                    if c >= 4:
                        pe.wait_ge(so_added, i * NC + (NC + c - 3))
                    mm(banks[:, OUT_BANKS[c % 4], 0:T], ynat[0:CAP, c * P:(c + 1) * P], GT[0:CAP, :],
                       start=True, stop=True).then_inc(so_ps, 1)

            norm_sums(4)
            for c in range(NC):
                h_chunk(4, c)
            for w in range(6):
                j, hf = divmod(w, 2)
                rows = P if j < 2 else TS
                for c in range(4):
                    last = tr(banks[0:rows, w, c * P:(c + 1) * P], hT[:, 4 * hf + c, j * P:j * P + rows], ident)
                last.then_inc(yt_ps, 1)

        @block.scalar
        def _(act):
            fn = nc.scalar.activation

            def norm(k):
                for half in range(2):
                    fn(sq[:, 4 * half:4 * half + 4], xT[:, 4 * half:4 * half + 4], ACT.Square).then_inc(sq_ready, 1)
                act.wait_ge(ms_ready, k + 1)
                fn(rms[:, :], banks[:, 7, 0:T], ACT.Sqrt, bias=eps[:, 0:1], scale=1.0 / D).then_inc(rms_ready, 1)

            for c in range(1, NC, 2):
                act.wait_ge(xt_ps, c + 1)
                nc.scalar.copy(xT[:, c], banks[:, c, 0:T]).then_inc(xt_act, 1)
            act.wait_ge(xt_act, 4)
            act.wait_ge(xt_dve, 4)
            act.wait_ge(eps_ready, 1)
            norm(0)
            for hf in range(2):
                act.wait_ge(st_ps, hf + 1)
                nc.scalar.copy(stT_f[:, 480 * hf:480 * (hf + 1)], banks[:, hf, 0:480]).then_inc(st_sb, 1)
            for hf in range(2):
                act.wait_ge(po_ps, hf + 1)
                nc.scalar.copy(pool_out[0:POOL_BUF + TS, 512 * hf:512 * (hf + 1)],
                               banks[0:POOL_BUF + TS, 5 + hf, :]).then_inc(po_sb, 1)
            act.wait_ge(pool_added, NC)
            norm(1)
            for u in range(FS * NG):
                act.wait_ge(gu_ps, u + 1)
                if u >= 2:
                    act.wait_ge(hid_done, u - 1)
                fn(sg[:, u % 2], banks[:, u % 2, 0:T], ACT.Silu).then_inc(silu_done, 1)
            act.wait_ge(ffn_added, NC * NG)
            norm(2)
            for n in range(0, N_PROJ, 2):
                act.wait_ge(proj_ps, n + 1)
                if n < 12:
                    nc.scalar.copy(zkv[:, n], banks[:, n % 4, 0:T]).then_inc(proj_act, 1)
                elif n < 20:
                    nc.scalar.mul(qT[:, (n - 12) // GQA, (n - 12) % GQA], banks[:, n % 4, 0:T], SCALE).then_inc(proj_act, 1)
                else:
                    nc.scalar.copy(gz[0:48, :], banks[0:48, n % 4, 0:T]).then_inc(proj_act, 1)
            for w in range(0, 9, 2):
                act.wait_ge(nat_ps, w + 1)
                j, quad = divmod(w, 3)
                dst = kvn[:, j, 512 * quad:512 * (quad + 1)] if j < 2 else kvs[0:TS, 512 * quad:512 * (quad + 1)]
                nc.scalar.copy(dst, banks[0:(P if j < 2 else TS), 4 + w % 4, :]).then_inc(nat_act, 1)
            act.wait_ge(gates_ps, 1)
            fn(gn[:, 0:2], banks[:, 5, 0:96].rearrange("p (j n) -> p j n", j=2), ACT.Exp, scale=-1.0)
            fn(gn[0:TS, 2], banks[0:TS, 5, 96:144], ACT.Exp, scale=-1.0).then_inc(gate_e, 1)
            act.wait_ge(cs_in, 1)
            fn(pcp_f, pcp_f, ACT.Exp).then_inc(cs_exp, 1)
            for n in range(0, UNITS, 2):
                act.wait_ge(kt_ps, n + 1)
                if n >= 2:
                    act.wait_ge(sc_done, n - 1)
                nc.scalar.copy(KT[:, n % 2], banks[:, 4 + n % 2, :]).then_inc(kt_act, 1)
            act.wait_ge(pcT_ps, 1)
            nc.scalar.copy(pcT, banks[:, 7, 0:TP]).then_inc(pcT_sb, 1)
            act.wait_ge(dec_max, 1)
            fn(sc_c, sc_c, ACT.Exp, bias=sm[:, 0:1], accum_out=sm[:, 3:4]).then_inc(dec_exp, 1)
            act.wait_ge(dec_max, 2)
            fn(sc_s, sc_s, ACT.Exp, bias=sm[:, 1:2], accum_out=sm[:, 4:5])
            fn(sc_w, sc_w, ACT.Exp, bias=sm[:, 2:3], accum_out=sm[:, 5:6]).then_inc(dec_exp, 1)
            for n in range(33):
                if n < 32:
                    act.wait_ge(ps_max, n + 1)
                    width = P * (n % 2 + 1)
                    for r in range(2):
                        last = fn(PR[:, n % 2, r, 0:width], PR[:, n % 2, r, 0:width], ACT.Exp,
                                  bias=pst[:, 4 * (n % 2) + r:4 * (n % 2) + r + 1],
                                  accum_out=pst[:, 8 + 2 * (n % 2) + r:9 + 2 * (n % 2) + r])
                    last.then_inc(ps_exp, 1)
                if n:
                    q = n - 1
                    width = 2 * P * (q % 2 + 1)
                    act.wait_ge(pt_ps, q + 1)
                    if q >= 2:
                        act.wait_ge(pv_done, q - 1)
                    nc.scalar.copy(PT[:, q % 2, 0:width], banks[:, 2 + q % 2, 0:width]).then_inc(pt_sb, 1)
            act.wait_ge(pv_done, 32)
            for q in range(4):
                act.wait_ge(vcn_ps, q + 1)
                nc.scalar.copy(vcn[0:NCMP_D, 2 * q:2 * q + 2].rearrange("p b n -> p (b n)"),
                               banks[0:NCMP_D, q, :]).then_inc(vcn_sb, 1)
            act.wait_ge(wo_added, NC)
            norm(3)
            for w in range(0, 6, 2):
                act.wait_ge(xn_ps, w + 1)
                nc.scalar.copy(xn[0:CAP, w // 2, 0:512], banks[0:CAP, w, :]).then_inc(xn_act, 1)
            act.wait_ge(top_gap, 1)
            fn(one[0:CAP, 6:9], one[0:CAP, 6:9], ACT.Exp).then_inc(top_exp, 1)

            def xe_copies():
                for hf in range(2):
                    nc.scalar.copy(xe[:, 4 * hf:4 * hf + 4].rearrange("p c s -> p (c s)"),
                                   banks[:, 6 + hf, 0:4 * CAP]).then_inc(xe_sb, 1)

            act.wait_ge(table_ready, 1)
            count = act.value_load(n_items[0:1, 0:1], min_val=NE, max_val=MAXI)
            act.wait_ge(xe_ps, 1)
            xe_copies()
            with act.Fori(0, count) as i:
                for g in range(NG):
                    act.wait_ge(mgu_ps, i * NG + (g + 1))
                    if g:
                        act.wait_ge(mhid, i * NG + g)
                    fn(msg, banks[:, g % 2, 0:FS * CAP], ACT.Silu).then_inc(msilu, 1)
                act.wait_ge(mdn_ps, i * NG + NG)
                for hf in range(2):
                    nc.scalar.copy(ysb[:, 4 * hf:4 * hf + 4].rearrange("p c s -> p (c s)"),
                                   banks[:, 4 + hf, 0:4 * CAP]).then_inc(ysb_done, 1)
                act.wait_ge(xe_ps, i + 2)
                xe_copies()
            act.wait_ge(so_added, count * NC + NC)
            norm(4)
            for w in range(0, 6, 2):
                act.wait_ge(yt_ps, w + 1)
                rows = P if w < 4 else TS
                nc.scalar.copy(yout[0:rows, w // 2, 0:512], banks[0:rows, w, :]).then_inc(yt_sb, 1)

        @block.vector
        def _(dve):
            V = nc.vector
            tt, ts, stt, red = V.tensor_tensor, V.tensor_scalar, V.scalar_tensor_tensor, V.tensor_reduce
            step = Steps(dve, dve_steps)

            def norm(k, v):
                dve.wait_ge(rms_ready, k + 1)
                step(V.reciprocal(rstd[:, :], rms[:, :]))
                step.settle()
                for c in range(NC):
                    stt(hT[:, c], xT[:, c], vecT[:, v, c:c + 1], rstd[:, :], ALU.mult, ALU.mult).then_inc(h_ready, 1)

            V.memset(eps[:, :], EPS).then_inc(eps_ready, 1)
            for c in range(0, NC, 2):
                dve.wait_ge(xt_ps, c + 1)
                V.tensor_copy(xT[:, c], banks[:, c, 0:T]).then_inc(xt_dve, 1)
            dve.wait_ge(vec_ps, 1)
            V.tensor_copy(vecT[:, :, :].rearrange("p v c -> p (v c)"), banks[:, 2, 0:48]).then_inc(vec_sb, 1)
            dve.wait_ge(vec_sb, 1)
            dve.wait_ge(xt_dve, 4)
            dve.wait_ge(xt_act, 4)
            norm(0, V_MIX0)
            dve.wait_ge(wkT_ps, 1)
            V.tensor_copy(wkT[:, :, :, :].rearrange("p a s c -> p (a s c)"), banks[:, 4, 0:128]).then_inc(wkT_sb, 1)
            tt(wb[:, :, :, :].rearrange("p s k n -> p (s k) n"),
               bc(wn[:, :, :].rearrange("p s k -> p (s k)"), 2, 4), bc(K("quarter"), 1, 8), ALU.mult).then_inc(wb_ready, 1)

            dve.wait_ge(h_ready, NC)
            dve.wait_ge(ms_ready, 1)
            h = hT[:, :, 0:TP]
            for src, dst, shift in ((h, s2, 1), (s2[:, 2:8], s4, 2), (s4[:, 2:6], s8, 4), (s8[:, 2:4], s16, 8)):
                step(tt(dst[:, :, shift:], src[:, :, shift:], src[:, :, 0:TP - shift], ALU.add))
                step(V.tensor_copy(dst[:, :, 0:shift], src[:, :, 0:shift]))
                step.settle()
            dve.wait_ge(st_sb, 2)
            for g, (s, w) in enumerate(zip((s2, s4[:, 0:2], s8[:, 0:2], s16), POOL_WINDOWS)):
                cs = slice(2 * g, 2 * g + 2)
                s = s[:, 0:2]
                step(stt(pl[:, cs, 0:TP], s, 1.0 / w, h[:, cs], ALU.mult, ALU.subtract))
                e = edge_f[:, 0:2 * (w - 1)].rearrange("p (c t) -> p c t", c=2)
                step(tt(e, s[:, :, 0:w - 1], bc(K("inv_cnt")[:, 0:w - 1], 1, 2), ALU.mult))
                step(red(ssum, stT[:, cs, :, 16 - w:], AX, ALU.add))
                step.settle()
                step(tt(pl[:, cs, 0:w - 1], e, h[:, cs, 0:w - 1], ALU.subtract))
                step(tt(ssum, ssum, hT[:, cs, TP:T], ALU.add))
                step.settle()
                stt(pl[:, cs, TP:T], ssum, 1.0 / w, hT[:, cs, TP:T], ALU.mult, ALU.subtract).then_inc(pooled, 1)
                dve.wait_ge(pooled, g + 1)
            for c in range(NC):
                dve.wait_ge(mixed, c + 1)
                stt(xT[:, c], banks[:, c, 0:T], vecT[:, V_POOL, c:c + 1], xT[:, c], ALU.mult, ALU.add
                    ).then_inc(pool_added, 1)
            dve.wait_ge(pool_added, NC)
            dve.wait_ge(po_ps, 2)
            norm(1, V_FFN0)

            def dense_adds(g):
                for d in range(NC):
                    u = NC * g + d
                    dve.wait_ge(down_ps, u + 1)
                    if g:
                        dve.wait_ge(ffn_added, u - NC + 1)
                    tt(xT[:, d], banks[:, 4 + u % 4, 0:T], xT[:, d], ALU.add).then_inc(ffn_added, 1)

            for g in range(NG + 1):
                if g < NG:
                    for s in range(FS):
                        u = FS * g + s
                        dve.wait_ge(silu_done, u + 1)
                        if g >= 2 and s == 0:
                            dve.wait_ge(down_ps, NC * (g - 1))
                        tt(hid[:, g % 2, s], sg[:, u % 2], banks[:, 2 + u % 2, 0:T], ALU.mult).then_inc(hid_done, 1)
                if g:
                    dense_adds(g - 1)
            dve.wait_ge(ffn_added, NC * NG)
            norm(2, V_MIX1)

            def order_queries(q):
                wait_tile(dve, Q_TILE0 + q)
                src = slot_view(Q_SLOT0 + q, "up").rearrange("p c (k g d) -> p c k g d", k=2, g=GQA)
                dst = wq[q].rearrange("p (c g k d) -> p c g k d", c=NC, g=GQA, k=2)
                if q:
                    dve.wait_ge(wq_ready, 2)
                for k2 in range(2):
                    V.tensor_copy(dst[:, :, :, k2, :], src[:, :, k2]).then_inc(wq_ready, 1)

            dve.wait_ge(qz_zero, 1)
            order_queries(0)
            for n in range(1, N_PROJ, 2):
                if n == 7:
                    order_queries(1)
                dve.wait_ge(proj_ps, n + 1)
                if n < 12:
                    V.tensor_copy(zkv[:, n], banks[:, n % 4, 0:T]).then_inc(proj_dve, 1)
                else:
                    ts(qT[:, (n - 12) // GQA, (n - 12) % GQA], banks[:, n % 4, 0:T], SCALE, None, ALU.mult
                       ).then_inc(proj_dve, 1)
            for w in range(1, 9, 2):
                dve.wait_ge(nat_ps, w + 1)
                j, quad = divmod(w, 3)
                dst = kvn[:, j, 512 * quad:512 * (quad + 1)] if j < 2 else kvs[0:TS, 512 * quad:512 * (quad + 1)]
                V.tensor_copy(dst, banks[0:(P if j < 2 else TS), 4 + w % 4, :]).then_inc(nat_dve, 1)
            dve.wait_ge(proj_act, 10)
            dve.wait_ge(proj_dve, 10)
            qz0 = 12 * T + 8 * T
            for a in range(2):
                for k2 in range(2):
                    at = qz0 + a * TS * P + (2 * a + k2) * GQA
                    base = arena[HD * k2:HD * (k2 + 1), at:at + GQA]
                    dst = bass.AP(base.tensor, base.offset, [list(base.ap[0]), [P + NH, TS], [1, GQA]])
                    last = V.tensor_copy(dst, qT[HD * k2:HD * (k2 + 1), a, :, TP:T].rearrange("p g b -> p b g"))
            last.then_inc(qz_ready, 1)
            for s, (kind, dst) in enumerate(((KC_, kcp), (VC_, vcp))):
                for a in range(2):
                    at = (2 * s + a) * TP
                    step(tt(sc_s[:, at:at + TP].rearrange("p (n c) -> p n c", n=NCMP_P),
                            zkv[:, 2 * kind + a, 0:TP].rearrange("p (n c) -> p n c", n=NCMP_P),
                            bc(wkT[:, a, s, :], 1, NCMP_P), ALU.mult))
            step.settle()
            for s, dst in enumerate((kcp, vcp)):
                red(dst, sc_s[:, 2 * s * TP:2 * (s + 1) * TP].rearrange("p (a n c) -> p a n c", a=2, n=NCMP_P), AX,
                    ALU.add).then_inc(cp_ready, 1)
            dve.wait_ge(gate_e, 1)
            step(ts(gn[:, 0:2], gn[:, 0:2], 1.0, None, ALU.add))
            step(ts(gn[0:TS, 2], gn[0:TS, 2], 1.0, None, ALU.add))
            step.settle()
            step(V.reciprocal(gn[:, 0:2], gn[:, 0:2]))
            V.reciprocal(gn[0:TS, 2], gn[0:TS, 2]).then_inc(gates_ready, 1)
            dve.wait_ge(vcp_ps, 1)
            V.tensor_copy(vcn_p[0:NCMP_P, :], banks[0:NCMP_P, 7, 0:KVW]).then_inc(vcp_sb, 1)
            dve.wait_ge(cs_ps, 1)
            for k2 in range(2):
                pcv, bkv, cbv = (v.rearrange("p (i a k x) -> p i a k x", i=2, a=2, k=2)[:, :, :, k2]
                                 for v in (pcp_f, banks[:, 7 - k2, 256:512], K("cmp_bias")))
                step(tt(pcv, bkv, cbv, ALU.add))
            step.settle()
            pc3 = pcp_f.rearrange("p (x n) -> p x n", n=NCMP_P)
            step(red(spread[:, 0:32], pc3, AX, ALU.max))
            step.settle()
            tt(pc3, pc3, bc(spread[:, 0:32], 2, NCMP_P), ALU.subtract).then_inc(cs_in, 1)
            dve.wait_ge(rep_ps, 1)
            for a in range(2):
                src = bc(banks[:, 2, P * a:P * (a + 1)].rearrange("p (k d) -> p k d", k=2), 1, GQA)
                mask = bc(K("head_of")[:, 8 * a:8 * (a + 1)].rearrange("p (g k) -> p g k", g=GQA), 3, HD)
                tt(vcz[:, 4 * a:4 * (a + 1)].rearrange("p g (k d) -> p g k d", k=2), src, mask, ALU.mult
                   ).then_inc(vcz_ready, 1)
            dve.wait_ge(cs_exp, 1)
            for i in range(2):
                step(tt(pcp[:, i], pcp[:, i], bc(K("cmp_mask")[:, 8 * i:8 * (i + 1)], 1, NH), ALU.mult))
            step.settle()
            step(red(spread[:, 0:32], pc3, AX, ALU.add))
            step.settle()
            step(ts(spread[:, 0:32], spread[:, 0:32], 1e-30, None, ALU.max))
            step.settle()
            step(V.reciprocal(spread[:, 32:64], spread[:, 0:32]))
            step.settle()
            step(tt(spread[:, 0:32].rearrange("p (i h) -> p i h", i=2),
                    spread[:, 32:64].rearrange("p (i h) -> p i h", i=2), gn[:, 0:2, 0:NH], ALU.mult))
            step.settle()
            tt(pc3, pc3, bc(spread[:, 0:32], 2, NCMP_P), ALU.mult).then_inc(cs_w, 1)

            for n in range(1, UNITS, 2):
                dve.wait_ge(kt_ps, n + 1)
                if n >= 2:
                    dve.wait_ge(sc_done, n - 1)
                V.tensor_copy(KT[:, n % 2], banks[:, 4 + n % 2, :]).then_inc(kt_dve, 1)
                if n % 6 == 5:
                    b = n // 6
                    dve.wait_ge(comp_ps, 2 * b + 2)
                    if b >= 2:
                        dve.wait_ge(kc_used, b - 1)
                    for s in range(2):
                        at = s * 128
                        v = banks[:, 6 + b % 2, at:at + 128].rearrange("p (n a k q) -> p a n k q", n=NPAGE, a=2, k=2)
                        dst = (kcT[:, b % 2] if s == 0 else vcT[:, b]).rearrange("p a (n q) -> p a n q", n=NPAGE)
                        for k2 in range(2):
                            half = slice(HD * k2, HD * (k2 + 1))
                            last = V.tensor_copy(dst[half], v[half, :, :, k2, :])
                    last.then_inc(kc_sb, 1)

            dve.wait_ge(sc_done, UNITS)
            dve.wait_ge(kc_used, TS)
            slope = K("slope")
            for hf in range(2):
                step(stt(sc_s[:, 512 * hf:512 * (hf + 1)], K("dist_d")[:, 512 * hf:512 * (hf + 1)], slope,
                         banks[:, hf, :], ALU.mult, ALU.add))
            step(stt(sc_w[:, 0:WIN], K("dist_d")[:, PAST - WIN:], slope, banks[:, 2, :], ALU.mult, ALU.add))
            step.settle()
            step(V.memset(sc_w[:, 0:1], NEG))
            step(V.tensor_copy(sc_s[:, PAST:PAST + 1], banks[:, 3, 0:1]))
            step(V.tensor_copy(sc_w[:, WIN:WIN + 1], banks[:, 3, 1:2]))
            stt(sc_c, K("dist_c"), slope, banks[:, 3, 32:32 + NCMP_D], ALU.mult, ALU.add).then_inc(dec_read, 1)
            dve.wait_ge(dec_read, 1)
            red(sm[:, 0:1], sc_c, AX, ALU.max, negate=True).then_inc(dec_max, 1)
            dve.wait_ge(gd_ps, 1)
            step(tt(gd, banks[:, 6, 64:112].rearrange("p (r h) -> p r h", r=3), bc(K("is_head"), 1, 3), ALU.mult))
            step.settle()
            step(red(gdec, gd, AX, ALU.add))
            dve.wait_ge(dec_exp, 1)
            step(ts(sm[:, 3:4], sm[:, 3:4], 1e-30, None, ALU.max))
            step.settle()
            step(V.reciprocal(sm[:, 6:7], sm[:, 3:4]))
            step.settle()
            step(ts(sc_c, sc_c, sm[:, 6:7], None, ALU.mult))
            step.settle()
            red(sm16[:, 0:NSLC_D], sc_c.rearrange("p (j r) -> p j r", r=SLC // CMP), AX, ALU.add).then_inc(imp_in, 1)
            dve.wait_ge(imp_ps, 1)
            step(tt(sm16[:, 16:32], banks[:, 6, 0:NSLC_D], K("forced"), ALU.add))
            step.settle()
            step(red(sm[:, 7:8], sm16[:, 16:32], AX, ALU.min))
            step.settle()
            step(stt(sm16[:, 32:48], sm16[:, 16:32], sm[:, 7:8], K("order"), ALU.is_equal, ALU.mult))
            step.settle()
            step(red(sm[:, 8:9], sm16[:, 32:48], AX, ALU.max))
            step.settle()
            step(ts(sm16[:, 48:64], sm16[:, 32:48], sm[:, 8:9], NEG, ALU.is_equal, ALU.mult))
            step.settle()
            s3 = sc_s[:, 0:PAST].rearrange("p (j t) -> p j t", t=SLC)
            step(tt(s3, s3, bc(sm16[:, 48:64], 2, SLC), ALU.add))
            step.settle()
            step(red(sm[:, 1:2], sc_s, AX, ALU.max, negate=True))
            red(sm[:, 2:3], sc_w, AX, ALU.max, negate=True).then_inc(dec_max, 1)
            dve.wait_ge(dec_exp, 2)
            step(V.reciprocal(sm[:, 9:11], sm[:, 4:6]))
            step.settle()
            step(tt(sm[:, 11:13], sm[:, 9:11], gdec[:, 1:3], ALU.mult))
            step.settle()
            step(ts(sc_c, sc_c, gdec[:, 0:1], None, ALU.mult))
            step(ts(sc_s, sc_s, sm[:, 11:12], None, ALU.mult))
            step(ts(sc_w, sc_w, sm[:, 12:13], None, ALU.mult))
            step.settle()
            step(ts(pn[:, 0, :], K("is_b"), sc_s[:, PAST:PAST + 1], None, ALU.mult))
            ts(pn[:, 1, :], K("is_b"), sc_w[:, WIN:WIN + 1], None, ALU.mult).then_inc(dprob, 1)

            def head(n):
                m, r = divmod(n, 4)
                a, g = divmod(m, GQA)
                k2, i = divmod(r, 2)
                return (2 * a + k2) * GQA + g, i

            def prompt_max(n):
                hd, i = head(n)
                width = P * (i + 1)
                dve.wait_ge(ps_ps, n + 1)
                if n >= 2:
                    dve.wait_ge(pt_ps, n - 1)
                else:
                    dve.wait_ge(sc_done, UNITS)
                stt(PR[:, n % 2, :, 0:width], bc(K("dist_p")[:, TP - width:TP], 1, 2), float(SLOPES[hd]),
                    banks[:, 4 + n % 2, :].rearrange("p (r t) -> p r t", r=2)[:, :, 0:width], ALU.mult, ALU.add
                    ).then_inc(ps_in, 1)
                dve.wait_ge(ps_in, n + 1)
                red(pst[:, 4 * (n % 2):4 * (n % 2) + 2], PR[:, n % 2, :, 0:width], AX, ALU.max, negate=True
                    ).then_inc(ps_max, 1)

            def prompt_weights(n):
                hd, i = head(n)
                width = P * (i + 1)
                o = n % 2
                dve.wait_ge(ps_exp, n + 1)
                step(V.reciprocal(pst[:, 12 + 2 * o:14 + 2 * o], pst[:, 8 + 2 * o:10 + 2 * o]))
                step.settle()
                step(tt(pst[:, 4 * o + 2:4 * o + 4], pst[:, 12 + 2 * o:14 + 2 * o],
                        gn[:, i, NH:3 * NH].rearrange("p (r h) -> p r h", r=2)[:, :, hd], ALU.mult))
                step.settle()
                tt(PR[:, o, :, 0:width], PR[:, o, :, 0:width], bc(pst[:, 4 * o + 2:4 * o + 4], 2, width), ALU.mult
                   ).then_inc(pw_ready, 1)

            for n in range(33 + 2):
                if n < 32:
                    prompt_max(n)
                if 1 <= n < 33:
                    prompt_weights(n - 1)
                if n >= 3 and (n - 3) % 4 == 3:
                    m = (n - 3) // 4
                    dve.wait_ge(pv_done, 4 * m + 4)
                    V.tensor_copy(hT[:, m, 0:TP], banks[:, m % 2, 0:TP]).then_inc(o_sb, 1)
            for q, (dst, rows, c0, width) in enumerate(((PsT_f[:, 0:512], P, 0, 512), (PsT_f[:, 512:1024], P, 0, 512),
                                                        (PwT_f, P, 0, 512))):
                dve.wait_ge(pdt_ps, q + 1)
                V.tensor_copy(dst, banks[:, 4 + q, :]).then_inc(pdt_sb, 1)
            dve.wait_ge(pdt_ps, 4)
            V.tensor_copy(PcT[0:NCMP_D, :], banks[0:NCMP_D, 7, 0:P]).then_inc(pdt_sb, 1)
            V.tensor_copy(PnT_f[0:TS, :], banks[0:TS, 7, P:3 * P]).then_inc(pdt_sb, 1)
            dve.wait_ge(od_ps, TS)
            for a in range(2):
                for k2 in range(2):
                    half = slice(HD * k2, HD * (k2 + 1))
                    v = banks[half, 2, P * a:P * (a + 1)].rearrange("p (b k g) -> p k g b", b=TS, k=NKV)
                    last = V.tensor_copy(hT[half, 4 * a:4 * (a + 1), TP:T], v[:, 2 * a + k2])
            last.then_inc(od_sb, 1)
            for c in range(NC):
                dve.wait_ge(wo_ps, c + 1)
                tt(xT[:, c], banks[:, 4 + c % 4, 0:T], xT[:, c], ALU.add).then_inc(wo_added, 1)
            dve.wait_ge(wo_added, NC)
            norm(3, V_FFN1)

            for w in range(1, 6, 2):
                dve.wait_ge(xn_ps, w + 1)
                V.tensor_copy(xn[0:CAP, w // 2, 512:1024], banks[0:CAP, w, :]).then_inc(xn_dve, 1)
            R = slice(0, CAP)
            top = one[R]
            dve.wait_ge(stored, 16 * 9)
            dve.wait_ge(lg_ps, 1)
            step(V.tensor_copy(lg[R], banks[R, 6, 0:NTC * NE].rearrange("p (j e) -> p j e", j=NTC)))
            step.settle()
            order3 = bc(K("e_order", CAP), 1, NTC)
            for r, (src, oh) in enumerate(((lg, oh1), (l2, oh2))):
                m = top[:, 3 * r:3 * r + 3]
                step(red(m, src[R], AX, ALU.max))
                step.settle()
                step(tt(eq[R], src[R], bc(m, 2, NE), ALU.is_equal))
                step.settle()
                step(tt(eq[R], eq[R], order3, ALU.mult))
                step.settle()
                step(red(top[:, 9:12], eq[R], AX, ALU.max))
                step.settle()
                step(tt(oh[R], eq[R], bc(top[:, 9:12], 2, NE), ALU.is_equal))
                step.settle()
                if r == 0:
                    step(stt(l2[R], oh1[R], NEG, lg[R], ALU.mult, ALU.add))
                    step.settle()
            step(tt(sel[R], oh1[R], oh2[R], ALU.add))
            step.settle()
            tt(top[:, 6:9], top[:, 3:6], top[:, 0:3], ALU.subtract).then_inc(top_gap, 1)
            V.tensor_copy(sel[R], sel[R]).then_inc(sel_ready, 1)
            dve.wait_ge(top_exp, 1)
            step(ts(top[:, 12:15], top[:, 6:9], 1.0, None, ALU.add))
            step.settle()
            step(V.reciprocal(top[:, 15:18], top[:, 12:15]))
            step.settle()
            step(tt(top[:, 18:21], top[:, 15:18], top[:, 6:9], ALU.mult))
            step(tt(oh1[R], oh1[R], bc(top[:, 15:18], 2, NE), ALU.mult))
            step.settle()
            step(tt(oh2[R], oh2[R], bc(top[:, 18:21], 2, NE), ALU.mult))
            step.settle()
            for r in range(3):
                step(tt(gx[R, :, r], oh1[R], oh2[R], ALU.add))
            dve.wait_ge(pos_ps, 1)
            step(stt(l2[R], banks[R, 6, 32:32 + NTC * NE].rearrange("p (j e) -> p j e", j=NTC), 1.0, sel[R], ALU.add,
                     ALU.mult))
            step.settle()
            for r in range(3):
                step(ts(posx[R, :, r], l2[R], -1.0 - r * CAP, None, ALU.add))
            step.settle()
            for r in range(2):
                step(V.tensor_copy(ovr[0:1, NE * r:NE * (r + 1)], banks[0:1, 6, 64:64 + NE]))
            step(V.tensor_copy(items_f[0:1, 0:MAXI + 1], K("items0", 1)))
            step.settle()
            step(tt(ovr[0:1, 16:32], ovr[0:1, 0:16], K("over_min", 1), ALU.is_gt))
            step.settle()
            step(tt(ovr[0:1, 32:48], ovr[0:1, 16:32], K("over_code", 1), ALU.mult))
            step(red(ovr[0:1, 48:49], ovr[0:1, 16:32], AX, ALU.add))
            step.settle()
            step(V.max(items_f[0:1, NE:2 * NE], ovr[0:1, 32:48]))
            step(ts(ovr[0:1, 49:50], ovr[0:1, 48:49], float(NE), None, ALU.add))
            step.settle()
            V.tensor_copy(items[0:1, :], items_f[0:1, 0:MAXI + 1]).then_inc(so_added, NC)
            dve.wait_ge(so_added, NC)
            V.tensor_copy(n_items[0:1, :], ovr[0:1, 49:50]).then_inc(table_ready, 1)
            dve.wait_ge(table_ready, 1)
            step.settle()
            count = dve.value_load(n_items[0:1, 0:1], min_val=NE, max_val=MAXI)

            def code_of(i):
                return dve.value_load(items[0:1, i:i + 1] if isinstance(i, int) else items[0:1, bass.ds(i, 1)],
                                      min_val=0, max_val=3 * NE - 1)

            def places(code):
                for j in range(NTC):
                    last = ts(Pm[R, j], K("iota_s", CAP), posc[R, j, bass.ds(code, 1)], None, ALU.is_equal)
                last.then_inc(P_ready, 1)

            places(code_of(0))
            with dve.Fori(0, count) as i:
                for g in range(NG):
                    dve.wait_ge(msilu, i * NG + (g + 1))
                    if g >= 2:
                        dve.wait_ge(mdn_ps, i * NG + (g - 1))
                    tt(mh[:, g % 2].rearrange("p f s -> p (f s)"), msg, banks[:, 2 + g % 2, 0:FS * CAP], ALU.mult
                       ).then_inc(mhid, 1)
                    if g == 0:
                        code = code_of(i)
                        for j in range(NTC):
                            last = ts(Gm[R, j], K("iota_s", CAP), posc[R, j, bass.ds(code, 1)],
                                      gxc[R, j, bass.ds(code, 1)], ALU.is_equal, ALU.mult)
                        last.then_inc(G_ready, 1)
                    if g == 1:
                        places(code_of(i + 1))
                dve.wait_ge(gt_ps, i + 1)
                V.tensor_copy(GT[R], banks[R, 1, 0:T]).then_inc(gt_sb, 1)
                for hf in range(2):
                    dve.wait_ge(yn_ps, i * 2 + (hf + 1))
                    V.tensor_copy(ynat[R, 512 * hf:512 * (hf + 1)], banks[R, 2 + hf, :]).then_inc(yn_sb, 1)
                for c in range(NC):
                    dve.wait_ge(so_ps, i * NC + (c + 1))
                    tt(xT[:, c], banks[:, (6, 7, 1, 3)[c % 4], 0:T], xT[:, c], ALU.add).then_inc(so_added, 1)
            dve.wait_ge(so_added, count * NC + NC)
            norm(4, V_FINAL)
            for w in range(1, 6, 2):
                dve.wait_ge(yt_ps, w + 1)
                rows = P if w < 4 else TS
                V.tensor_copy(yout[0:rows, w // 2, 512:1024], banks[0:rows, w, :]).then_inc(yt_sb, 1)


INPUTS = ["x_prompt", "x_sample", "state_pool", "cache_kv", "state_win", "page_table", "norm_mix", "w_pool",
          "pool_scale", "w_nsa_in", "w_cmp_k", "w_cmp_v", "w_nsa_out", "norm_ffn", "w_ffn_gate", "w_ffn_up",
          "w_ffn_down", "w_router", "w_moe_gate", "w_moe_up", "w_moe_down", "norm_final"]
OUTPUTS = [(1, TP, D), (TS, 1, D), (1, 1, POOL_BUF, D), (1, TS, POOL_BUF, D), (1, 1, TP, 4, NKV, HD),
           (1, TS, 1, 4, NKV, HD), (1, 1, TP, 2, NKV, HD), (1, TS, WIN, 2, NKV, HD)]


def kernel(**inputs):
    import concourse.bacc as bacc
    from concourse.bass_utils import run_bass_kernel_spmd as run

    nc = bacc.Bacc("TRN2", target_bir_lowering=False, num_devices=1)
    arrays, args = {}, []
    for name in INPUTS:
        a = np.ascontiguousarray(inputs[name])
        arrays["in_" + name] = a
        args.append(nc.dram_tensor("in_" + name, a.shape, mybir.dt.from_np(a.dtype), kind="ExternalInput").ap())
    table = np.concatenate(list(constants().values()), axis=1)
    arrays["in_consts"] = table
    args.append(nc.dram_tensor("in_consts", table.shape, F32, kind="ExternalInput").ap())
    for i, shape in enumerate(OUTPUTS):
        args.append(nc.dram_tensor(f"out_{i}", shape, F32, kind="ExternalOutput").ap())
    build(nc, *args)
    r = run(nc, [arrays], core_ids=[0])
    return tuple(r.results[0][f"out_{i}"] for i in range(len(OUTPUTS)))
```

```python
from contextlib import ExitStack

import numpy as np

import concourse.bass as bass
from concourse import mybir

F32 = mybir.dt.float32
I32 = mybir.dt.int32
ALU = mybir.AluOpType
ACT = mybir.ActivationFunctionType
AX = mybir.AxisListType.X

P = 128
D = 1024
NC = D // P
TP = 256
TS = 8
T = TP + TS
EPS = 1e-6
NEG = -1e30
POOL_WINDOWS = (2, 4, 8, 16)
POOL_BUF = 15
NH, NKV, GQA, HD = 16, 4, 4, 64
KVW = NKV * HD
QW = NH * HD
PAST = 1024
PAGE = 128
NPAGE = PAST // PAGE
CMP = 32
NCMP_P = TP // CMP
NCMP_D = PAST // CMP
SLC = 64
NSLC_D = PAST // SLC
WIN = 512
FORCE = 1000.0
SCALE = HD ** -0.5
DFF = 3584
NE = 8
FG = 512
NG = DFF // FG
FS = FG // P
NSLOT = 7
TILE = NC * FG
CAP = T // 3
NTC = 3
MAXI = NE + 8
EXPERT_TILES = 3 * NG
USES_BEFORE = 4
SLOPES = np.exp2(-8.0 * np.arange(1, NH + 1, dtype=np.float32) / NH).astype(np.float32)


def constants():
    p = np.arange(P)
    f = np.float32
    out = {}
    out["ident"] = np.eye(P)
    out["ones"] = np.ones((P, P))
    t = np.arange(TP)[None, :]
    out["dist_p"] = np.where(t <= P + p[:, None], t - (P + p[:, None]), NEG)
    out["dist_d"] = np.broadcast_to(np.arange(PAST) - PAST, (P, PAST))
    mid = np.arange(NCMP_D) * CMP + (CMP - 1) / 2
    out["dist_c"] = np.broadcast_to(mid - PAST, (P, NCMP_D))
    out["slope"] = SLOPES[p % NH][:, None]
    i, n = np.arange(2)[None, :, None, None], np.arange(NCMP_P)[None, None, None, :]
    tq = i * P + p[:, None, None, None]
    ok = (n + 1) * CMP - 1 <= tq
    sl = SLOPES[None, None, :, None]
    out["cmp_bias"] = np.where(ok, -sl * (tq - (n * CMP + (CMP - 1) / 2)), NEG + 0 * sl).reshape(P, -1)
    out["cmp_mask"] = ok.reshape(P, -1)
    kp, g, k2 = np.arange(2)[:, None, None], np.arange(4)[None, :, None], np.arange(2)[None, None, :]
    out["head_of"] = (p[:, None, None, None] // NCMP_P == (2 * kp + k2) * GQA + g).reshape(P, -1)
    out["blk_of"] = (p[None, :] % NCMP_P == p[:, None])
    out["inv_cnt"] = np.broadcast_to(1.0 / (np.arange(15) + 1), (P, 15))
    out["same_kv"] = p[:, None] // GQA == p[None, :] // GQA
    forced = np.zeros(NSLC_D)
    forced[[0, NSLC_D - 1]] = FORCE
    out["forced"] = np.broadcast_to(forced, (P, NSLC_D))
    out["order"] = np.broadcast_to(np.arange(NSLC_D) + 1, (P, NSLC_D))
    out["is_head"] = p[:, None] % NH == np.arange(NH)[None, :]
    out["spread_b"] = p[:, None] == p[None, :] // NH
    out["is_b"] = p[:, None] // NH == np.arange(TS)[None, :]
    out["iota_s"] = np.broadcast_to(np.arange(CAP), (P, CAP))
    out["before"] = p[:, None] < np.arange(CAP)[None, :]
    out["e_order"] = np.broadcast_to(NE - np.arange(NE), (P, NE))
    out["k_rows"] = (p[:, None, None] == (2 * np.arange(2)[None, :, None] + p[None, None, :] // HD)).reshape(P, -1)
    out["quarter"] = p[:, None] // CMP == np.arange(4)[None, :]
    out["over_code"] = np.broadcast_to(np.arange(NE, 3 * NE), (P, 2 * NE))
    out["over_min"] = np.broadcast_to(np.repeat([CAP, 2 * CAP], NE), (P, 2 * NE))
    out["items0"] = np.broadcast_to(np.arange(MAXI + 1) * (np.arange(MAXI + 1) < NE), (P, MAXI + 1))
    return {k: np.asarray(v, dtype=f) for k, v in out.items()}


def const_columns():
    at, cols = 0, {}
    for name, a in constants().items():
        cols[name] = (at, a.shape[1])
        at += a.shape[1]
    return cols, at


class Steps:

    def __init__(self, eng, sem):
        self.eng, self.sem, self.n, self.per, self.it = eng, sem, 0, 0, None

    def __call__(self, ins):
        ins.then_inc(self.sem, 1)
        self.n += 1

    def settle(self):
        if self.it is None:
            self.eng.wait_ge(self.sem, self.n)
        else:
            self.eng.wait_ge(self.sem, self.it * self.per + self.n)

    def loop(self, it, per):
        self.it, self.per, self.start = it, per, self.n

    def end(self):
        assert self.n - self.start == self.per, (self.n - self.start, self.per)
        self.it = None


def bc(ap, axis, n):
    shape = list(ap.shape)
    shape.insert(axis, n)
    return ap.unsqueeze(axis).to_broadcast(shape)


def build(nc, x_prompt, x_sample, state_pool, cache_kv, state_win, page_table, norm_mix, w_pool, pool_scale,
          w_nsa_in, w_cmp_k, w_cmp_v, w_nsa_out, norm_ffn, w_ffn_gate, w_ffn_up, w_ffn_down, w_router,
          w_moe_gate, w_moe_up, w_moe_down, norm_final, consts,
          y_prompt, y_sample, new_pool_prompt, new_pool_sample, new_kv_prompt, new_kv_sample, new_win_prompt,
          new_win_sample):
    ctx = ExitStack()
    with ctx:
        def sb(name, shape, dt=F32):
            return ctx.enter_context(nc.sbuf_tensor(name, shape, dt))

        def sem(name):
            return ctx.enter_context(nc.semaphore(name))

        mm = nc.tensor.matmul
        tr = nc.tensor.transpose

        Q_SLOT0 = (EXPERT_TILES + 3) % NSLOT

        cols, n_const = const_columns()
        cst = sb("cst", [P, n_const])

        def K(name, rows=P):
            a, n = cols[name]
            return cst[0:rows, a:a + n]

        ident = K("ident")
        ones = K("ones")
        ring = sb("ring", [P, NSLOT, TILE])
        xT = sb("xT", [P, NC, T])
        hT = sb("hT", [P, NC, T])
        vec_rows = sb("vec_rows", [48, P])
        vecT = sb("vecT", [P, 6, NC])
        V_MIX0, V_MIX1, V_FFN0, V_FFN1, V_FINAL, V_POOL = range(6)
        router = sb("router", [P, NC, NE])
        w_gates = sb("w_gates", [P, NC, 48])
        rms = sb("rms", [P, T])
        rstd = sb("rstd", [P, T])
        pages = sb("pages", [1, TS * NPAGE], I32)
        wn = sb("wn", [P, 2, NKV])
        wcT = sb("wcT", [NKV, 2, CMP])
        wkT = sb("wkT", [P, 2, 2, CMP])
        wb = sb("wb", [P, 2, NKV, 4])
        AR = 15800
        arena = sb("arena", [P, AR])
        banks = ctx.enter_context(nc.psum_tensor("banks", [P, 8, 512], F32))

        def carve(base, *sizes):
            out, at = [], 0
            for n in sizes:
                out.append(base[:, at:at + n])
                at += n
            assert at <= base.shape[1], (at, base.shape)
            return out

        early = ring[:, 5:7, :].rearrange("p s n -> p (s n)")
        x_nat_f, xs_nat, st_nat, wpool_f, stT_f = carve(early, 2 * D, D, D, 2 * D, NC * TS * POOL_BUF)
        x_nat = x_nat_f.rearrange("p (j d) -> p j d", j=2)
        wpool = wpool_f.rearrange("p (g c e) -> p g c e", g=4, c=2)
        stT = stT_f.rearrange("p (c b j) -> p c b j", c=NC, b=TS)
        sq_f, s2_f, s4_f, s8_f, s16_f, pl_f, pool_out, edge_f, ssum_f = carve(
            arena[:, :], NC * T, 8 * TP, 6 * TP, 4 * TP, 2 * TP, NC * T, D, 30, 16)
        sq = sq_f.rearrange("p (c t) -> p c t", c=NC)
        s2, s4, s8, s16 = (a.rearrange("p (c t) -> p c t", t=TP) for a in (s2_f, s4_f, s8_f, s16_f))
        pl = pl_f.rearrange("p (c t) -> p c t", c=NC)
        ssum = ssum_f.rearrange("p (c b) -> p c b", c=2)
        _, hid_f, sg_f = carve(arena[:, :], NC * T, 2 * FS * T, 2 * T)
        hid = hid_f.rearrange("p (s f t) -> p s f t", s=2, f=FS)
        sg = sg_f.rearrange("p (s t) -> p s t", s=2)
        (zkv_f, qT_f, qz_f, kvn_f, kvs, sc_s, sc_w, sc_c, gn_f, pcp_f, kcp_f, vcp_f, vcz_f, pcT, sm,
         sm16, gd_f, gdec, pn_f, spread, qa_f, kcz_f) = carve(
            arena[:, :], 12 * T, 8 * T, 2048, 3072, 1536, PAST + 1, WIN + 1, NCMP_D, 3 * 48, 256, 16, 16,
            1024, 256, 16, 64, 48, 3, 2 * TS, 64, 2 * P, 4 * NCMP_P)
        wq = [arena[:, 20 * T + 2048:20 * T + 2048 + TILE], ring[:, Q_SLOT0, :]]
        gz = rms
        vcn_p = sc_w[:, 0:KVW]
        zkv = zkv_f.rearrange("p (c t) -> p c t", c=12)
        KC_, VC_, KS_, VS_, KW_, VW_ = range(6)
        qT = qT_f.rearrange("p (a g t) -> p a g t", a=2, g=GQA)
        qz = qz_f.rearrange("p (a b m) -> p a b m", a=2, b=TS)
        qa = qa_f.rearrange("p (a m) -> p a m", a=2)
        kcz = kcz_f.rearrange("p (a k n) -> p a k n", a=2, k=2)
        kvn = kvn_f.rearrange("p (j n) -> p j n", j=2)
        gn = gn_f.rearrange("p (j n) -> p j n", j=3)
        pcp = pcp_f.rearrange("p (i h n) -> p i h n", i=2, h=NH)
        kcp = kcp_f.rearrange("p (a n) -> p a n", a=2)
        vcp = vcp_f.rearrange("p (a n) -> p a n", a=2)
        vcz = vcz_f.rearrange("p (m n) -> p m n", m=8)
        gd = gd_f.rearrange("p (r h) -> p r h", r=3)
        pn = pn_f.rearrange("p (r b) -> p r b", r=2)
        late = ring[:, 0:3, :].rearrange("p s n -> p (s n)")
        kb0, kb1, kb2, kt_f, kw_f, vcT_f, kcT_f = carve(late, 3072, 3072, 3072, 1024, 1024, 512, 128)
        kbuf = [kb0, kb1, kb2]
        KT = kt_f.rearrange("p (s t) -> p s t", s=2)
        KWn = kw_f.rearrange("p (c n) -> p c n", c=4)
        vcT = vcT_f.rearrange("p (b a n) -> p b a n", b=TS, a=2)
        kcT = kcT_f.rearrange("p (s a n) -> p s a n", s=2, a=2)
        PR_f, PT_f, pst_f, odn = carve(ring[:, (Q_SLOT0 + 1) % NSLOT, :], 4 * 512, 3 * 512, 4 * 8, KVW)
        PR = PR_f.rearrange("p (s r t) -> p s r t", s=4, r=2)
        PT = PT_f.rearrange("p (s t) -> p s t", s=3)
        pst = pst_f.rearrange("p (s n r) -> p s n r", s=4, n=4)
        NEG_MAX, SUM, INV_SUM, WEIGHT = range(4)
        vcn = late[:, 9216:9216 + 2048].rearrange("p (b n) -> p b n", b=TS)
        PsT_f, PwT_f, PcT, PnT_f = carve(qz_f, 1024, 512, 128, 256)
        PsT = PsT_f.rearrange("p (c m) -> p c m", c=8)
        PwT = PwT_f.rearrange("p (c m) -> p c m", c=4)
        PnT = PnT_f.rearrange("p (r m) -> p r m", r=2)
        (_, xn_f, xe_f, mh_f, msg, ynat, Pm_f, Gm_f, GT, lg_f, l2_f, eq_f, oh1_f, oh2_f, sel_f, gate_f,
         posx_f, gx_f, one, ovr, items_f, yout_f) = carve(
            arena[:, :], NC * T, NTC * D, NC * CAP, 2 * FS * CAP, FS * CAP, D, T, T, T, 24, 24, 24, 24, 24,
            24, 24, 72, 72, 24, 64, 24, 3 * D)
        xn = xn_f.rearrange("p (j d) -> p j d", j=NTC)
        xe = xe_f.rearrange("p (c s) -> p c s", c=NC)
        mh = mh_f.rearrange("p (b f s) -> p b f s", b=2, f=FS)
        Pm, Gm = (a.rearrange("p (j s) -> p j s", j=NTC) for a in (Pm_f, Gm_f))
        lg, l2, eq, oh1, oh2, sel, gate = (a.rearrange("p (j e) -> p j e", j=NTC)
                                           for a in (lg_f, l2_f, eq_f, oh1_f, oh2_f, sel_f, gate_f))
        posx, gx = (a.rearrange("p (j r e) -> p j r e", j=NTC, r=3) for a in (posx_f, gx_f))
        posc, gxc = (a.rearrange("p (j c) -> p j c", j=NTC) for a in (posx_f, gx_f))
        yout = yout_f.rearrange("p (j d) -> p j d", j=3)
        items = sb("items", [1, MAXI + 1], I32)
        n_items = sb("n_items", [1, 1], I32)
        eps = sb("eps", [P, 1])

        consts_in, vecs_in, xin, xsin, states_in, wpool_in, router_in, wgates_in, wcmp_in, pages_in = (
            sem(n) for n in ("consts_in", "vecs_in", "xin", "xsin", "states_in", "wpool_in", "router_in", "wgates_in",
                             "wcmp_in", "pages_in"))
        tile_in = [sem(f"tile_in{s}") for s in range(NSLOT)]
        kb_in = [sem(f"kb_in{i}") for i in range(3)]
        stored, rows_moved, kw_in = sem("stored"), sem("rows_moved"), sem("kw_in")
        xt_ps, xt_act, xt_dve, st_ps, st_sb, vec_ps, vec_sb, wkT_ps, wkT_sb, wb_ready = (
            sem(n) for n in ("xt_ps", "xt_act", "xt_dve", "st_ps", "st_sb", "vec_ps", "vec_sb", "wkT_ps", "wkT_sb",
                             "wb_ready"))
        sq_ready, ms_ready, rms_ready, h_ready = (sem(n) for n in ("sq_ready", "ms_ready", "rms_ready", "h_ready"))
        po_ps, po_sb, pooled, mixed, pool_added = (sem(n) for n in ("po_ps", "po_sb", "pooled", "mixed", "pool_added"))
        gu_ps, silu_done, hid_done, down_ps, ffn_added = (sem(n) for n in (
            "gu_ps", "silu_done", "hid_done", "down_ps", "ffn_added"))
        proj_ps, proj_act, proj_dve, nat_ps, nat_act, nat_dve, gates_ps, gate_e, gates_ready = (sem(n) for n in (
            "proj_ps", "proj_act", "proj_dve", "nat_ps", "nat_act", "nat_dve", "gates_ps", "gate_e", "gates_ready"))
        qz_zero, qz_ready, cp_ready, vcp_ps, vcp_sb, rep_ps, vcz_ready, cs_ps, cs_in, cs_exp, cs_w, pcT_ps, pcT_sb = (
            sem(n) for n in ("qz_zero", "qz_ready", "cp_ready", "vcp_ps", "vcp_sb", "rep_ps", "vcz_ready", "cs_ps",
                             "cs_in", "cs_exp", "cs_w", "pcT_ps", "pcT_sb"))
        kt_ps, kt_act, kt_dve, sc_done, comp_ps, kc_sb, kc_used = (sem(n) for n in (
            "kt_ps", "kt_act", "kt_dve", "sc_done", "comp_ps", "kc_sb", "kc_used"))
        dec_read, dec_max, dec_exp, imp_in, imp_ps, gd_ps, dprob = (sem(n) for n in (
            "dec_read", "dec_max", "dec_exp", "imp_in", "imp_ps", "gd_ps", "dprob"))
        ps_ps, ps_in, ps_max, ps_exp, pw_ready, pt_ps, pt_sb, pv_done, o_sb = (sem(n) for n in (
            "ps_ps", "ps_in", "ps_max", "ps_exp", "pw_ready", "pt_ps", "pt_sb", "pv_done", "o_sb"))
        vcn_ps, vcn_sb, pdt_ps, pdt_sb, od_ps, od_sb, wo_ps, wo_added = (sem(n) for n in (
            "vcn_ps", "vcn_sb", "pdt_ps", "pdt_sb", "od_ps", "od_sb", "wo_ps", "wo_added"))
        xn_ps, xn_act, xn_dve, lg_ps, top_gap, top_exp, sel_ready, pos_ps, table_ready = (sem(n) for n in (
            "xn_ps", "xn_act", "xn_dve", "lg_ps", "top_gap", "top_exp", "sel_ready", "pos_ps", "table_ready"))
        P_ready, G_ready, xe_ps, xe_sb, mgu_ps, msilu, mhid, mdn_ps = (sem(n) for n in (
            "P_ready", "G_ready", "xe_ps", "xe_sb", "mgu_ps", "msilu", "mhid", "mdn_ps"))
        gt_ps, gt_sb, yn_sb, so_ps, so_added, yt_ps, yt_act, yt_dve, y_stored = (sem(n) for n in (
            "gt_ps", "gt_sb", "yn_sb", "so_ps", "so_added", "yt_ps", "yt_act", "yt_dve",
            "y_stored"))
        od_nat, odt_ps = sem("od_nat"), sem("odt_ps")
        ident_in = sem("ident_in")
        dve_steps, eps_ready, wq_ready = sem("dve_steps"), sem("eps_ready"), sem("wq_ready")

        KV_TILE0 = EXPERT_TILES
        Q_TILE0 = KV_TILE0 + 3
        O_TILE0 = Q_TILE0 + 2
        assert O_TILE0 + 2 == USES_BEFORE * NSLOT
        N_PROJ = 21
        UNITS = 6 * TS

        def slot_view(s, shape):
            if shape == "up":
                return ring[:, s, :].rearrange("p (c f) -> p c f", c=NC)
            return ring[:, s, :].rearrange("p (q n) -> p q n", q=FS)

        def extra(s):
            return 16 if s in (O_TILE0 % NSLOT, (O_TILE0 + 1) % NSLOT) else 0

        def wait_tile(eng, t):
            eng.wait_ge(tile_in[t % NSLOT], 16 * (t // NSLOT + 1) + (16 if t >= O_TILE0 else 0))

        def wait_expert_tile(eng, i, j):
            s, u = j % NSLOT, j // NSLOT
            eng.wait_ge(tile_in[s], i * (16 * 3) + (16 * (USES_BEFORE + u + 1) + extra(s)))

        def ffn_tile(wg, wu, wd, j):
            g, kind = divmod(j, 3)
            if kind < 2:
                w = (wg, wu)[kind]
                return w.rearrange("(c p) f -> p c f", p=P)[:, :, g * FG:(g + 1) * FG], "up"
            return wd.rearrange("(q p) n -> p q n", p=P)[:, g * FS:(g + 1) * FS, :], "down"

        def kb_value(n):
            return sum(16 * (4 if m < 2 * TS else 9) for m in range(n % 3, n + 1, 3))

        GCOL = QW + 6 * KVW
        w_in_v = w_nsa_in[0].rearrange("(c p) n -> p c n", p=P)
        block = ctx.enter_context(nc.Block())

        @block.sync
        def _(sp):
            sp.dma_start(cst[:, 0:2 * P], consts[:, 0:2 * P]).then_inc(ident_in, 16)
            sp.dma_start(x_nat, x_prompt[0].rearrange("(j p) d -> p j d", p=P)).then_inc(xin, 16)
            sp.dma_start(xs_nat[0:TS, :], x_sample.rearrange("b q d -> (b q) d")).then_inc(xsin, 16)
            for n, v in enumerate((norm_mix[0], norm_mix[1], norm_ffn[0], norm_ffn[1], norm_final, pool_scale[0])):
                sp.dma_start(vec_rows[8 * n:8 * n + 8, :], v.rearrange("(c p) -> c p", p=P)).then_inc(vecs_in, 16)
            sp.dma_start(st_nat[0:TS * POOL_BUF, :], state_pool[0].rearrange("b j d -> (b j) d")).then_inc(states_in, 16)
            sp.dma_start(cst[:, 2 * P:], consts[:, 2 * P:]).then_inc(consts_in, 16)
            for g in range(4):
                sp.dma_start(wpool[:, g], w_pool[0, g].rearrange("(c p) e -> p c e", p=P)).then_inc(wpool_in, 16)

            for t in range(EXPERT_TILES + 5):
                if t < NSLOT:
                    if t == 5:
                        sp.wait_ge(mixed, NC)
                else:
                    g, kind = divmod(t - NSLOT, 3)
                    if kind < 2:
                        sp.wait_ge(gu_ps, FS * (g + 1))
                    else:
                        sp.wait_ge(down_ps, NC * (g + 1))
                s = t % NSLOT
                if t < EXPERT_TILES:
                    src, shape = ffn_tile(w_ffn_gate[0], w_ffn_up[0], w_ffn_down[0], t)
                elif t < Q_TILE0:
                    c0 = QW + (t - KV_TILE0) * FG
                    src, shape = w_in_v[:, :, c0:c0 + FG], "up"
                else:
                    c0 = (t - Q_TILE0) * FG
                    src, shape = w_in_v[:, :, c0:c0 + FG], "up"
                sp.dma_start(slot_view(s, shape), src).then_inc(tile_in[s], 16)
                if t == 4:
                    sp.dma_start(router[:, :, :], w_router[0].rearrange("(c p) e -> p c e", p=P)).then_inc(router_in, 16)
                    sp.dma_start(w_gates[:, :, :], w_in_v[:, :, GCOL:GCOL + 48]).then_inc(wgates_in, 16)
                    sp.dma_start(pages[0:1, :], page_table.rearrange("(o b) p -> o (b p)", o=1)).then_inc(pages_in, 16)
                if t == 8:
                    sp.dma_start(new_win_sample[0, :, 0:WIN - 1].rearrange("b w s k d -> b (w s k d)"),
                                 state_win[0, :, 1:WIN].rearrange("b w s k d -> b (w s k d)")).then_inc(rows_moved, 16)
            for n in range(2):
                t = O_TILE0 + n
                g, kind = divmod(t - NSLOT, 3)
                sp.wait_ge(down_ps if kind == 2 else gu_ps, (NC if kind == 2 else FS) * (g + 1))
                for k2 in range(2):
                    r0 = (2 * n + k2) * GQA * HD
                    sp.dma_start(slot_view(t % NSLOT, "down")[HD * k2:HD * (k2 + 1)],
                                 w_nsa_out[0, r0:r0 + GQA * HD].rearrange("(g d) n -> d g n", d=HD)
                                 ).then_inc(tile_in[t % NSLOT], 16)

            sp.wait_ge(proj_ps, 12)
            sp.wait_ge(pages_in, 16)

            def load_pages(b, half, dst, c0, c1, done):
                for n in range(4):
                    at = b * NPAGE + half * 4 + n
                    pid = sp.value_load(pages[0:1, at:at + 1], min_val=0, max_val=cache_kv.shape[1] - 1)
                    src = cache_kv[0, bass.ds(pid, 1)].rearrange("o t s k d -> (o t) (s k d)")
                    sp.dma_start(dst[:, n], src[:, c0:c1]).then_inc(done, 16)

            def expert_tile(i, j, weights):
                s = j % NSLOT
                if j >= NSLOT or not isinstance(i, int):
                    g, kind = divmod(j - NSLOT if j >= NSLOT else j + 2 * NSLOT, 3)
                    back = 0 if j >= NSLOT else NG
                    sp.wait_ge(mgu_ps if kind < 2 else mdn_ps, i * NG + (g + 1 - back))
                src, shape = ffn_tile(*weights, j)
                sp.dma_start(slot_view(s, shape), src).then_inc(tile_in[s], 16)

            first = [w[0, 0] for w in (w_moe_gate, w_moe_up, w_moe_down)]
            for b in range(TS):
                for half in range(2):
                    n = 2 * b + half
                    if n >= 3:
                        sp.wait_ge(comp_ps, n - 2)
                    load_pages(b, half, kbuf[n % 3].rearrange("p (n c) -> p n c", n=4), 0, 3 * KVW, kb_in[n % 3])
                if b:
                    sp.wait_ge(kt_ps, 6 * b)
                sp.dma_start(KWn, state_win[0, b, :, 0].rearrange("(c p) k d -> p c (k d)", p=P)).then_inc(kw_in, 16)
                if b == 2:
                    sp.wait_ge(proj_ps, N_PROJ - 1)
                    expert_tile(0, 3, first)
            for b in range(TS):
                n = 2 * TS + b
                if b < 3:
                    sp.wait_ge(comp_ps, n - 2)
                else:
                    sp.wait_ge(od_ps, b - 2)
                for half in range(2):
                    load_pages(b, half, kbuf[n % 3][:, half * 1024:(half + 1) * 1024].rearrange("p (n c) -> p n c", n=4),
                               3 * KVW, 4 * KVW, kb_in[n % 3])
                sp.dma_start(kbuf[n % 3][:, 2048:3072].rearrange("p (c n) -> p c n", c=4),
                             state_win[0, b, :, 1].rearrange("(c p) k d -> p c (k d)", p=P)).then_inc(kb_in[n % 3], 16)
            sp.wait_ge(od_ps, TS)
            for j in range(3):
                expert_tile(0, j, first)
            sp.wait_ge(odt_ps, TS)
            expert_tile(0, 4, first)
            sp.wait_ge(wo_ps, NC)
            for j in range(5, EXPERT_TILES):
                expert_tile(0, j, first)

            def dyn(w, e):
                return w[0, bass.ds(e, 1)].rearrange("o a b -> (o a) b")

            with sp.Fori(1, NE) as i:
                for j in range(EXPERT_TILES):
                    expert_tile(i, j, [dyn(w, i) for w in (w_moe_gate, w_moe_up, w_moe_down)])
            sp.wait_ge(table_ready, 1)
            count = sp.value_load(n_items[0:1, 0:1], min_val=NE, max_val=MAXI)
            with sp.If(count > NE):
                with sp.Fori(NE, count) as i:
                    code = sp.value_load(items[0:1, bass.ds(i, 1)], min_val=0, max_val=3 * NE - 1)
                    e = sp.snap(code % NE, min_val=0, max_val=NE - 1)
                    for j in range(EXPERT_TILES):
                        expert_tile(i, j, [dyn(w, e) for w in (w_moe_gate, w_moe_up, w_moe_down)])
            sp.wait_ge(rows_moved, 16)
            for j in range(3):
                sp.wait_ge(yt_act, j + 1)
                sp.wait_ge(yt_dve, j + 1)
                if j < 2:
                    sp.dma_start(y_prompt[0, j * P:(j + 1) * P], yout[:, j, :]).then_inc(y_stored, 16)
                else:
                    sp.dma_start(y_sample.rearrange("b q d -> (b q) d"), yout[0:TS, 2, :]).then_inc(y_stored, 16)
            sp.wait_ge(y_stored, 16 * 3)
            sp.wait_ge(stored, 16 * 9)

        @block.gpsimd
        def _(gp):
            for s, w in enumerate((w_cmp_k, w_cmp_v)):
                for q in range(4):
                    gp.dma_start(wn[CMP * q:CMP * (q + 1), s, :], w[0]).then_inc(wcmp_in, 16)
            with nc.allow_non_contiguous_dma(reason="256 numbers"):
                for s, w in enumerate((w_cmp_k, w_cmp_v)):
                    gp.dma_start(wcT[:, s, :], w[0].rearrange("c k -> k c")).then_inc(wcmp_in, 16)
            gp.dma_start(new_pool_sample[0, :, 0:POOL_BUF - 1], state_pool[0, :, 1:POOL_BUF]).then_inc(stored, 16)
            gp.wait_ge(po_sb, 2)
            gp.dma_start(new_pool_prompt[0, 0], pool_out[0:POOL_BUF, :]).then_inc(stored, 16)
            gp.dma_start(new_pool_sample[0, :, POOL_BUF - 1], pool_out[POOL_BUF:POOL_BUF + TS, :]).then_inc(stored, 16)
            gp.wait_ge(mixed, NC)
            gp.wait_ge(stored, 16 * 3)
            gp.memset(qz_f, 0.0).then_inc(qz_zero, 1)
            gp.memset(qa_f, 0.0).then_inc(qz_zero, 1)
            gp.memset(kcz_f, 0.0).then_inc(qz_zero, 1)
            gp.wait_ge(nat_act, 5)
            gp.wait_ge(nat_dve, 4)
            for j in range(2):
                rows = slice(j * P, (j + 1) * P)
                gp.dma_start(new_kv_prompt[0, 0, rows].rearrange("t s k d -> t (s k d)"), kvn[:, j, 0:4 * KVW]
                             ).then_inc(stored, 16)
                gp.dma_start(new_win_prompt[0, 0, rows].rearrange("t s k d -> t (s k d)"), kvn[:, j, 4 * KVW:]
                             ).then_inc(stored, 16)
            gp.dma_start(new_kv_sample[0].rearrange("b q s k d -> (b q) (s k d)"), kvs[0:TS, 0:4 * KVW]
                         ).then_inc(stored, 16)
            gp.dma_start(new_win_sample[0, :, WIN - 1].rearrange("b s k d -> b (s k d)"), kvs[0:TS, 4 * KVW:]
                         ).then_inc(stored, 16)

        @block.tensor
        def _(pe):
            def norm_sums(k):
                for c in range(NC):
                    pe.wait_ge(sq_ready, NC * k + c + 1)
                    last = mm(banks[:, 0, 0:T], ones, sq[:, c], start=(c == 0), stop=(c == NC - 1))
                last.then_inc(ms_ready, 1)

            def h_chunk(k, c):
                pe.wait_ge(h_ready, NC * k + c + 1)

            def keep_clock(n, bank):
                for _ in range(n):
                    mm(banks[:, bank, :], ones, cst[:, 0:512], start=True, stop=True)

            pe.wait_ge(ident_in, 16)
            pe.wait_ge(xin, 16)
            pe.wait_ge(xsin, 16)
            for c in range(NC):
                for j in range(2):
                    tr(banks[:, c, j * P:(j + 1) * P], x_nat[:, j, c * P:(c + 1) * P], ident)
                tr(banks[:, c, TP:T], xs_nat[0:TS, c * P:(c + 1) * P], ident[0:TS, 0:TS]).then_inc(xt_ps, 1)
            pe.wait_ge(vecs_in, 6 * 16)
            pe.wait_ge(xt_dve, 3)
            tr(banks[:, 2, 0:48], vec_rows[:, :], ident[0:48, 0:48]).then_inc(vec_ps, 1)
            norm_sums(0)
            n_state = TS * POOL_BUF
            pe.wait_ge(states_in, 16)
            for c in range(NC):
                last = tr(banks[:, 1 + 2 * (c // 4), (c % 4) * n_state:(c % 4 + 1) * n_state],
                          st_nat[0:n_state, c * P:(c + 1) * P], ident[0:n_state, 0:n_state])
                if c % 4 == 3:
                    last.then_inc(st_ps, 1)
            pe.wait_ge(xt_dve, 4)
            for c in range(NC):
                h_chunk(0, c)
                last = tr(banks[0:POOL_BUF + TS, 5 + c // 4, (c % 4) * P:(c % 4 + 1) * P],
                          hT[:, c, TP - POOL_BUF:T], ident)
                if c % 4 == 3:
                    last.then_inc(po_ps, 1)
            pe.wait_ge(consts_in, 16)
            keep_clock(4, 7)
            pe.wait_ge(wpool_in, 4 * 16)
            pe.wait_ge(st_sb, 2)
            pe.wait_ge(vec_sb, 1)
            pe.wait_ge(xt_dve, 3)
            pe.wait_ge(po_sb, 2)
            for g in range(4):
                pe.wait_ge(pooled, g + 1)
                for e in range(2):
                    for c in range(2):
                        last = mm(banks[:, 2 * g + e, 0:T], wpool[:, g, c, e * P:(e + 1) * P], pl[:, 2 * g + c],
                                  start=(c == 0), stop=(c == 1))
                    last.then_inc(mixed, 1)
            norm_sums(1)
            keep_clock(3, 7)

            def dense_up(g):
                for s in range(FS):
                    u = FS * g + s
                    if u >= 2:
                        pe.wait_ge(hid_done, u - 1)
                    for kind in range(2):
                        t = 3 * g + kind
                        if s == 0:
                            wait_tile(pe, t)
                        w = slot_view(t % NSLOT, "up")
                        for c in range(NC):
                            if u == 0 and kind == 0:
                                h_chunk(1, c)
                            last = mm(banks[:, 2 * kind + u % 2, 0:T], w[:, c, s * P:(s + 1) * P], hT[:, c],
                                      start=(c == 0), stop=(c == NC - 1))
                    last.then_inc(gu_ps, 1)

            def dense_down(g):
                if g == 0:
                    pe.wait_ge(wkT_sb, 1)
                t = 3 * g + 2
                wait_tile(pe, t)
                pe.wait_ge(hid_done, FS * (g + 1))
                w = slot_view(t % NSLOT, "down")
                for d in range(NC):
                    u = NC * g + d
                    if u >= 4:
                        pe.wait_ge(ffn_added, u - 3)
                    for s in range(FS):
                        last = mm(banks[:, 4 + u % 4, 0:T], w[:, s, d * P:(d + 1) * P], hid[:, g % 2, s],
                                  start=(s == 0), stop=(s == FS - 1))
                    last.then_inc(down_ps, 1)

            for g in range(NG + 1):
                if g < NG:
                    dense_up(g)
                if g == 0:
                    pe.wait_ge(wcmp_in, 10 * 16)
                    pe.wait_ge(pool_added, 5)
                    for a in range(2):
                        last = mm(banks[:, 4, 64 * a:64 * (a + 1)], K("k_rows", NKV)[:, P * a:P * (a + 1)],
                                  wcT[:, :, :].rearrange("k s c -> k (s c)"), start=True, stop=True)
                    last.then_inc(wkT_ps, 1)
                if g:
                    dense_down(g - 1)
            norm_sums(2)

            for n in range(N_PROJ):
                if n >= 4:
                    pe.wait_ge(proj_dve if n % 2 else proj_act, (n - 4) // 2 + 1)
                if n in (12, 16):
                    pe.wait_ge(wq_ready, 2 * ((n - 12) // 4 + 1))
                if n == N_PROJ - 1:
                    pe.wait_ge(wgates_in, 16)
                    w, rows = w_gates[:, :, :], 48
                else:
                    t = KV_TILE0 + n // 4
                    if n % 4 == 0 and n < 12:
                        wait_tile(pe, t)
                    w, rows = slot_view(t % NSLOT, "up"), P
                for c in range(NC):
                    if n == 0:
                        h_chunk(2, c)
                    if n == N_PROJ - 1:
                        lhs = w[:, c, :]
                    elif n < 12:
                        lhs = w[:, c, (n % 4) * P:(n % 4 + 1) * P]
                    else:
                        at = c * FG + (n - 12) % GQA * P
                        lhs = wq[(n - 12) // GQA][:, at:at + P]
                    last = mm(banks[0:rows, n % 4, 0:T], lhs, hT[:, c], start=(c == 0), stop=(c == NC - 1))
                last.then_inc(proj_ps, 1)
            pe.wait_ge(cp_ready, 3)
            for a in range(2):
                last = tr(banks[0:NCMP_P, 7, P * a:P * (a + 1)], vcp[:, a, :], ident)
            last.then_inc(vcp_ps, 1)
            pe.wait_ge(proj_act, 6)
            pe.wait_ge(proj_dve, 6)
            for w in range(9):
                j, quad = divmod(w, 3)
                rows = P if j < 2 else TS
                if w == 3:
                    pe.wait_ge(vcp_sb, 1)
                if w >= 4:
                    pe.wait_ge(nat_dve if w % 2 else nat_act, (w - 4) // 2 + 1)
                for c in range(4):
                    last = tr(banks[0:rows, 4 + w % 4, c * P:(c + 1) * P], zkv[:, 4 * quad + c, j * P:j * P + rows],
                              ident)
                last.then_inc(nat_ps, 1)
            pe.wait_ge(proj_act, 11)
            pe.wait_ge(nat_dve, 3)
            for j in range(3):
                rows = P if j < 2 else TS
                last = tr(banks[0:rows, 5, 48 * j:48 * (j + 1)], gz[0:48, j * P:j * P + rows], ident[0:48, 0:48])
            last.then_inc(gates_ps, 1)
            pe.wait_ge(proj_act, 10)
            pe.wait_ge(proj_dve, 10)
            mm(banks[:, 2, 0:KVW], K("blk_of", NCMP_P), vcn_p[0:NCMP_P, :], start=True, stop=True).then_inc(rep_ps, 1)

            pe.wait_ge(qz_ready, 1)
            pe.wait_ge(wb_ready, 1)
            for r, kind in enumerate((KS_, KW_)):
                for a in range(2):
                    mm(banks[:, 3, TS * r:TS * (r + 1)], qa[:, a], zkv[:, 2 * kind + a, TP:T],
                       start=(r == 0 and a == 0), stop=(a == 1), skip_group_check=True)
            pe.wait_ge(nat_act, 5)
            pe.wait_ge(gate_e, 1)

            def key_unit(n):
                b, u = divmod(n, 6)
                if u < 4:
                    hf, a = divmod(u, 2)
                    m = 2 * b + hf
                    if a == 0:
                        pe.wait_ge(kb_in[m % 3], 64 * (m // 3 + 1))
                    src = kbuf[m % 3].rearrange("p (n c) -> p n c", n=4)[:, :, 2 * KVW + P * a:2 * KVW + P * (a + 1)]
                else:
                    a = u - 4
                    if a == 0:
                        pe.wait_ge(kw_in, 16 * (b + 1))
                    src = KWn[:, :, P * a:P * (a + 1)]
                if n >= 2:
                    pe.wait_ge(kt_dve if n % 2 else kt_act, (n - 2) // 2 + 1)
                for c in range(4):
                    last = tr(banks[:, 4 + n % 2, c * P:(c + 1) * P], src[:, c, :], ident)
                last.then_inc(kt_ps, 1)

            def prompt_compressed(quarter):
                a = quarter // 2
                if quarter == 0:
                    pe.wait_ge(kc_sb, 2)
                for g in range(2 * (quarter % 2), 2 * (quarter % 2) + 2):
                    for i in range(2):
                        at = ((a * GQA + g) * 2 + i) * 2 * NCMP_P
                        last = mm(banks[:, 7, at:at + 2 * NCMP_P], qT[:, a, g, i * P:(i + 1) * P],
                                  kcz[:, a].rearrange("p k n -> p (k n)"), start=True, stop=True)
                if quarter == 3:
                    last.then_inc(cs_ps, 1)

            def unit_scores(n):
                b, u = divmod(n, 6)
                a, bank = (u % 2, u // 2) if u < 4 else (u - 4, 2)
                pe.wait_ge(kt_dve if n % 2 else kt_act, n // 2 + 1)
                if n == 4:
                    pe.wait_ge(vcz_ready, 2)
                mm(banks[:, bank, :], qz[:, a, b], KT[:, n % 2], start=(b == 0 and a == 0),
                   stop=(b == TS - 1 and a == 1), skip_group_check=True).then_inc(sc_done, 1)

            def compress_half(m, s):
                b, hf = divmod(m, 2)
                if m == 6 and s == 0:
                    pe.wait_ge(cs_in, 1)
                if s == 0 and hf == 0 and b >= 2:
                    pe.wait_ge(kc_sb, b - 1)
                v = kbuf[m % 3].rearrange("p (n c) -> p n c", n=4)
                for pg in range(4):
                    for a in range(2):
                        at = ((s * NPAGE + 4 * hf + pg) * 2 + a) * 8
                        last = mm(banks[:, 6 + b % 2, at:at + 8], v[:, pg, s * KVW + P * a:s * KVW + P * (a + 1)],
                                  wb[:, s, 2 * a:2 * a + 2, :], start=True, stop=True)
                if s == 1:
                    last.then_inc(comp_ps, 1)

            def compressed_scores(b):
                pe.wait_ge(kc_sb, b + 1)
                for a in range(2):
                    last = mm(banks[:, 3, 32:32 + NCMP_D], qz[:, a, b], kcT[:, b % 2, a],
                              start=False, stop=(b == TS - 1 and a == 1), skip_group_check=True)
                last.then_inc(kc_used, 1)

            pe.wait_ge(nat_act, 4)
            pe.wait_ge(nat_dve, 4)
            keep_clock(3, 0)
            for n in range(UNITS):
                key_unit(n)
                if n:
                    unit_scores(n - 1)
                if 13 <= n <= 16:
                    prompt_compressed(n - 13)
                if 1 <= n % 6 <= 4:
                    compress_half(2 * (n // 6) + (n % 6 - 1) // 2, (n - 1) % 6 % 2)
                if n % 6 == 0 and n:
                    compressed_scores(n // 6 - 1)
            unit_scores(UNITS - 1)
            compressed_scores(TS - 1)

            pe.wait_ge(cs_w, 1)
            pe.wait_ge(kc_sb, TS)
            for i in range(2):
                last = tr(banks[:, 7, P * i:P * (i + 1)], pcp_f[:, P * i:P * (i + 1)], ident)
            last.then_inc(pcT_ps, 1)

            pe.wait_ge(gates_ready, 1)
            mm(banks[:, 6, 64:112], K("spread_b", TS), gn[0:TS, 2, :], start=True, stop=True).then_inc(gd_ps, 1)
            pe.wait_ge(dec_read, 1)
            for b in range(TS):
                for a in range(2):
                    n = 2 * b + a
                    last = tr(banks[0:NCMP_D, n // 4, (n % 4) * P:(n % 4 + 1) * P], vcT[:, b, a], ident)
                if b % 2:
                    last.then_inc(vcn_ps, 1)
            pe.wait_ge(imp_in, 1)
            mm(banks[:, 6, 0:NSLC_D], K("same_kv"), sm16[:, 0:NSLC_D], start=True, stop=True).then_inc(imp_ps, 1)
            def where(n):
                m, r = divmod(n, 4)
                a, g = divmod(m, GQA)
                k2, i = divmod(r, 2)
                return m, a, g, k2, i, slice(HD * k2, HD * (k2 + 1))

            def prompt_scores(n):
                m, a, g, k2, i, half = where(n)
                if n >= 2:
                    pe.wait_ge(ps_in, n - 1)
                for r, kind in enumerate((KS_, KW_)):
                    last = mm(banks[:, 4 + n % 2, 256 * r:256 * r + P * (i + 1)], qT[half, a, g, i * P:(i + 1) * P],
                              zkv[half, 2 * kind + a, 0:P * (i + 1)], start=True, stop=True)
                last.then_inc(ps_ps, 1)

            def prompt_transposes(n):
                i = n % 2
                pe.wait_ge(pw_ready, n + 1)
                if n >= 2:
                    pe.wait_ge(pt_sb, n - 1)
                for r in range(2):
                    for t in range(i + 1):
                        at = (r * (i + 1) + t) * P
                        last = tr(banks[:, 2 + n % 2, at:at + P], PR[:, n % 4, r, t * P:(t + 1) * P], ident)
                last.then_inc(pt_ps, 1)

            def prompt_values(n):
                m, a, g, k2, i, half = where(n)
                if n % 4 == 0:
                    if m >= 2:
                        pe.wait_ge(o_sb, m - 1)
                    mm(banks[:, m % 2, 0:TP], vcz[:, m], pcT, start=True, stop=False, skip_group_check=True)
                pe.wait_ge(pt_sb, n + 1)
                for r, kind in enumerate((VS_, VW_)):
                    for t in range(i + 1):
                        at = (r * (i + 1) + t) * P
                        c0 = kind * KVW + (2 * a + k2) * HD
                        last = mm(banks[half, m % 2, i * P:(i + 1) * P], kvn[:, t, c0:c0 + HD],
                                  PT[:, n % 3, at:at + P], start=False, stop=(r == 1 and t == i),
                                  skip_group_check=True)
                last.then_inc(pv_done, 1)

            def decode_values(b, quarter):
                n = 2 * TS + b
                if quarter == 0:
                    pe.wait_ge(kb_in[n % 3], kb_value(n))
                    if b >= 2:
                        pe.wait_ge(od_sb, b - 1)
                hs = slice(NH * b, NH * (b + 1))
                out = banks[0:NH, 6 + b % 2, 0:KVW]
                if quarter == 0:
                    for r, kind in enumerate((VS_, VW_)):
                        mm(out, PnT[0:TS, r, hs], kvs[0:TS, kind * KVW:(kind + 1) * KVW], start=(r == 0), stop=False)
                    mm(out, PcT[0:NCMP_D, hs], vcn[0:NCMP_D, b, :], start=False, stop=False)
                for c in range(3 * quarter, 3 * quarter + 3):
                    prob = PsT[:, c, hs] if c < 8 else PwT[:, c - 8, hs]
                    last = mm(out, prob, kbuf[n % 3][:, c * KVW:(c + 1) * KVW], start=False, stop=(c == 11))
                if quarter == 3:
                    last.then_inc(od_ps, 1)

            def decode_outputs(b):
                pe.wait_ge(od_nat, b + 1)
                for a in range(2):
                    last = tr(banks[:, 6 + b % 2, KVW + NH * a:KVW + NH * (a + 1)], odn[0:NH, P * a:P * (a + 1)],
                              ident[0:NH, 0:NH])
                last.then_inc(odt_ps, 1)

            pe.wait_ge(pcT_sb, 1)
            for n in range(36):
                if n < 32:
                    prompt_scores(n)
                if n == 1:
                    keep_clock(7, 7)
                    pe.wait_ge(vcn_sb, 4)
                    pe.wait_ge(dprob, 1)
                    for c in range(8):
                        last = tr(banks[:, c // 4, (c % 4) * P:(c % 4 + 1) * P], sc_s[:, c * P:(c + 1) * P], ident)
                        if c % 4 == 3:
                            last.then_inc(pdt_ps, 1)
                    for c in range(4):
                        last = tr(banks[:, 2, c * P:(c + 1) * P], sc_w[:, c * P:(c + 1) * P], ident)
                    last.then_inc(pdt_ps, 1)
                    tr(banks[0:NCMP_D, 3, 0:P], sc_c, ident)
                    for r in range(2):
                        last = tr(banks[0:TS, 3, P * (r + 1):P * (r + 2)], pn[:, r, :], ident)
                    last.then_inc(pdt_ps, 1)
                    pe.wait_ge(pdt_sb, 5)
                if 2 <= n < 34:
                    prompt_transposes(n - 2)
                if 3 <= n < 35:
                    prompt_values(n - 3)
                if 2 <= n < 34:
                    decode_values((n - 2) // 4, (n - 2) % 4)
                if n >= 7 and n % 4 == 3:
                    decode_outputs(n // 4 - 1)

            for c in range(2):
                wait_tile(pe, O_TILE0 + c)
            pe.wait_ge(od_sb, TS)
            pe.wait_ge(o_sb, 8)
            for c in range(NC):
                if c >= 4:
                    pe.wait_ge(wo_added, c - 3)
                for m in range(8):
                    a, g = divmod(m, GQA)
                    last = mm(banks[:, 4 + c % 4, 0:T],
                              slot_view((O_TILE0 + a) % NSLOT, "down")[:, g, c * P:(c + 1) * P], hT[:, m],
                              start=(m == 0), stop=(m == 7))
                last.then_inc(wo_ps, 1)
            norm_sums(3)
            pe.wait_ge(wo_added, 7)
            keep_clock(5, 6)

            for c in range(NC):
                h_chunk(3, c)
            pe.wait_ge(router_in, 16)
            for j in range(NTC):
                for c in range(NC):
                    last = mm(banks[0:CAP, 6, NE * j:NE * (j + 1)], hT[:, c, j * CAP:(j + 1) * CAP], router[:, c, :],
                              start=(c == 0), stop=(c == NC - 1))
            last.then_inc(lg_ps, 1)
            for w in range(6):
                j, hf = divmod(w, 2)
                for c in range(4):
                    last = tr(banks[0:CAP, w, c * P:(c + 1) * P], hT[:, 4 * hf + c, j * CAP:(j + 1) * CAP], ident)
                last.then_inc(xn_ps, 1)
            keep_clock(2, 7)
            pe.wait_ge(sel_ready, 1)
            for j in range(NTC):
                for q in range(j + 1):
                    mm(banks[0:CAP, 6, 32 + NE * j:32 + NE * (j + 1)],
                       K("before", CAP) if q == j else ones[0:CAP, 0:CAP], sel[0:CAP, q], start=(q == 0), stop=(q == j))
            for q in range(NTC):
                last = mm(banks[:, 6, 64:64 + NE], ones[0:CAP, :], sel[0:CAP, q], start=(q == 0), stop=(q == NTC - 1))
            last.then_inc(pos_ps, 1)

            def gather():
                for c in range(NC):
                    for j in range(NTC):
                        last = mm(banks[:, 6 + c // 4, (c % 4) * CAP:(c % 4 + 1) * CAP],
                                  xn[0:CAP, j, c * P:(c + 1) * P], Pm[0:CAP, j, :], start=(j == 0), stop=(j == NTC - 1))
                last.then_inc(xe_ps, 1)

            keep_clock(4, 7)
            pe.wait_ge(xn_act, 3)
            pe.wait_ge(xn_dve, 3)
            pe.wait_ge(table_ready, 1)
            count = pe.value_load(n_items[0:1, 0:1], min_val=NE, max_val=MAXI)
            pe.wait_ge(P_ready, 1)
            gather()
            keep_clock(1, 2)

            def expert_step(i, g):
                if g == 0:
                    pe.wait_ge(xe_sb, i * 2 + 2)
                if g == 1:
                    pe.wait_ge(so_added, i * NC + NC)
                if g >= 2:
                    pe.wait_ge(mhid, i * NG + (g - 1))
                behind = (() if g == 0 else (1, 2, 3, 4, 5) if g == NG - 1 else (1, 2, 3, 4, 5, 6, 7))
                down = 0
                for kind in range(2):
                    wait_expert_tile(pe, i, 3 * g + kind)
                    w = slot_view((3 * g + kind) % NSLOT, "up")
                    for s in range(FS):
                        for c in range(NC):
                            last = mm(banks[:, 2 * kind + g % 2, s * CAP:(s + 1) * CAP], w[:, c, s * P:(s + 1) * P],
                                      xe[:, c], start=(c == 0), stop=(c == NC - 1))
                        if kind == 1 and s == FS - 1:
                            last.then_inc(mgu_ps, 1)
                        if FS * kind + s in behind:
                            expert_down(i, g - 1, down, down + 1)
                            down += 1
                if g:
                    expert_down(i, g - 1, down, 2 * FS)

            def expert_down(i, g, first, end):
                if first == 0:
                    wait_expert_tile(pe, i, 3 * g + 2)
                    pe.wait_ge(mhid, i * NG + (g + 1))
                w = slot_view((3 * g + 2) % NSLOT, "down")
                for n in range(first, end):
                    hf, s = divmod(n, FS)
                    last = mm(banks[0:CAP, 4 + hf, :], mh[:, g % 2, s], w[:, s, 512 * hf:512 * (hf + 1)],
                              start=(g == 0 and s == 0), stop=(g == NG - 1 and s == FS - 1))
                    if n == 2 * FS - 1:
                        last.then_inc(mdn_ps, 1)

            OUT_BANKS = (6, 7, 1, 3)
            with pe.Fori(0, count) as i:
                for g in range(NG):
                    expert_step(i, g)
                expert_down(i, NG - 1, 0, 2 * FS)
                pe.wait_ge(P_ready, i + 2)
                gather()
                pe.wait_ge(G_ready, i + 1)
                for j in range(NTC):
                    last = tr(banks[0:CAP, 1, j * CAP:(j + 1) * CAP], Gm[0:CAP, j, :], ident[0:CAP, 0:CAP])
                last.then_inc(gt_ps, 1)
                pe.wait_ge(gt_sb, i + 1)
                pe.wait_ge(yn_sb, i * 2 + 2)
                pe.wait_ge(xe_sb, i * 2 + 4)
                for c in range(NC):
                    if c >= 4:
                        pe.wait_ge(so_added, i * NC + (NC + c - 3))
                    mm(banks[:, OUT_BANKS[c % 4], 0:T], ynat[0:CAP, c * P:(c + 1) * P], GT[0:CAP, :],
                       start=True, stop=True).then_inc(so_ps, 1)

            norm_sums(4)
            keep_clock(6, 7)
            for w in (0, 2, 4, 1, 3, 5):
                j, hf = divmod(w, 2)
                rows = P if j < 2 else TS
                if j == 0:
                    h_chunk(4, 4 * hf + 3)
                for c in range(4):
                    last = tr(banks[0:rows, w, c * P:(c + 1) * P], hT[:, 4 * hf + c, j * P:j * P + rows], ident)
                last.then_inc(yt_ps, 1)

        @block.scalar
        def _(act):
            fn = nc.scalar.activation

            def norm(k, added=None, base=0):
                for c in range(NC):
                    if added is None:
                        act.wait_ge(xt_act if c % 2 else xt_dve, c // 2 + 1)
                    else:
                        act.wait_ge(added, base + (c + 1))
                    fn(sq[:, c], xT[:, c], ACT.Square).then_inc(sq_ready, 1)
                act.wait_ge(ms_ready, k + 1)
                fn(rms[:, :], banks[:, 0, 0:T], ACT.Sqrt, bias=eps[:, 0:1], scale=1.0 / D).then_inc(rms_ready, 1)

            for c in range(1, NC, 2):
                act.wait_ge(xt_ps, c + 1)
                nc.scalar.copy(xT[:, c], banks[:, c, 0:T]).then_inc(xt_act, 1)
            act.wait_ge(eps_ready, 1)
            norm(0)
            for hf in range(2):
                act.wait_ge(st_ps, hf + 1)
                nc.scalar.copy(stT_f[:, 480 * hf:480 * (hf + 1)], banks[:, 1 + 2 * hf, 0:480]).then_inc(st_sb, 1)
            for hf in range(2):
                act.wait_ge(po_ps, hf + 1)
                nc.scalar.copy(pool_out[0:POOL_BUF + TS, 512 * hf:512 * (hf + 1)],
                               banks[0:POOL_BUF + TS, 5 + hf, :]).then_inc(po_sb, 1)
            norm(1, pool_added)
            for u in range(FS * NG):
                act.wait_ge(gu_ps, u + 1)
                if u >= 2:
                    act.wait_ge(hid_done, u - 1)
                fn(sg[:, u % 2], banks[:, u % 2, 0:T], ACT.Silu).then_inc(silu_done, 1)
            norm(2, ffn_added, NC * (NG - 1))
            for n in range(0, N_PROJ, 2):
                act.wait_ge(proj_ps, n + 1)
                if n < 12:
                    nc.scalar.copy(zkv[:, n], banks[:, n % 4, 0:T]).then_inc(proj_act, 1)
                elif n < 20:
                    nc.scalar.mul(qT[:, (n - 12) // GQA, (n - 12) % GQA], banks[:, n % 4, 0:T], SCALE).then_inc(proj_act, 1)
                else:
                    nc.scalar.copy(gz[0:48, :], banks[0:48, n % 4, 0:T]).then_inc(proj_act, 1)
            for w in range(0, 9, 2):
                act.wait_ge(nat_ps, w + 1)
                j, quad = divmod(w, 3)
                dst = kvn[:, j, 512 * quad:512 * (quad + 1)] if j < 2 else kvs[0:TS, 512 * quad:512 * (quad + 1)]
                nc.scalar.copy(dst, banks[0:(P if j < 2 else TS), 4 + w % 4, :]).then_inc(nat_act, 1)
            act.wait_ge(gates_ps, 1)
            fn(gn[:, 0:2], banks[:, 5, 0:96].rearrange("p (j n) -> p j n", j=2), ACT.Exp, scale=-1.0)
            fn(gn[0:TS, 2], banks[0:TS, 5, 96:144], ACT.Exp, scale=-1.0).then_inc(gate_e, 1)
            for n in range(0, UNITS, 2):
                act.wait_ge(kt_ps, n + 1)
                if n >= 2:
                    act.wait_ge(sc_done, n - 1)
                nc.scalar.copy(KT[:, n % 2], banks[:, 4 + n % 2, :]).then_inc(kt_act, 1)
                if n == 18:
                    act.wait_ge(cs_in, 1)
                    fn(pcp_f, pcp_f, ACT.Exp).then_inc(cs_exp, 1)
            act.wait_ge(pcT_ps, 1)
            nc.scalar.copy(pcT, banks[:, 7, 0:TP]).then_inc(pcT_sb, 1)
            act.wait_ge(dec_max, 1)
            fn(sc_c, sc_c, ACT.Exp, bias=sm[:, 0:1], accum_out=sm[:, 3:4]).then_inc(dec_exp, 1)
            for q in range(4):
                act.wait_ge(vcn_ps, q + 1)
                nc.scalar.copy(vcn[0:NCMP_D, 2 * q:2 * q + 2].rearrange("p b n -> p (b n)"),
                               banks[0:NCMP_D, q, :]).then_inc(vcn_sb, 1)
            act.wait_ge(dec_max, 2)
            fn(sc_s, sc_s, ACT.Exp, bias=sm[:, 1:2], accum_out=sm[:, 4:5])
            fn(sc_w, sc_w, ACT.Exp, bias=sm[:, 2:3], accum_out=sm[:, 5:6]).then_inc(dec_exp, 1)
            for q, dst in enumerate((PsT_f[:, 0:512], PsT_f[:, 512:1024], PwT_f)):
                act.wait_ge(pdt_ps, q + 1)
                nc.scalar.copy(dst, banks[:, q, :]).then_inc(pdt_sb, 1)
            act.wait_ge(pdt_ps, 4)
            nc.scalar.copy(PcT[0:NCMP_D, :], banks[0:NCMP_D, 3, 0:P]).then_inc(pdt_sb, 1)
            nc.scalar.copy(PnT_f[0:TS, :], banks[0:TS, 3, P:3 * P]).then_inc(pdt_sb, 1)
            for n in range(35):
                if n < 32:
                    act.wait_ge(ps_max, n + 1)
                    width = P * (n % 2 + 1)
                    for r in range(2):
                        last = fn(PR[:, n % 4, r, 0:width], PR[:, n % 4, r, 0:width], ACT.Exp,
                                  bias=pst[:, n % 4, NEG_MAX, r:r + 1], accum_out=pst[:, n % 4, SUM, r:r + 1])
                    last.then_inc(ps_exp, 1)
                if 2 <= n < 34:
                    q = n - 2
                    width = 2 * P * (q % 2 + 1)
                    act.wait_ge(pt_ps, q + 1)
                    if q >= 3:
                        act.wait_ge(pv_done, q - 2)
                    nc.scalar.copy(PT[:, q % 3, 0:width], banks[:, 2 + q % 2, 0:width]).then_inc(pt_sb, 1)
                if n >= 6 and n % 4 == 2:
                    b = n // 4 - 1
                    act.wait_ge(od_ps, b + 1)
                    if b:
                        act.wait_ge(odt_ps, b)
                    nc.scalar.copy(odn[0:NH, :], banks[0:NH, 6 + b % 2, 0:KVW]).then_inc(od_nat, 1)
            norm(3, wo_added)
            for w in range(0, 6, 2):
                act.wait_ge(xn_ps, w + 1)
                nc.scalar.copy(xn[0:CAP, w // 2, 0:512], banks[0:CAP, w, :]).then_inc(xn_act, 1)
            act.wait_ge(top_gap, 1)
            fn(one[0:CAP, 6:9], one[0:CAP, 6:9], ACT.Exp).then_inc(top_exp, 1)

            def xe_copies():
                for hf in range(2):
                    nc.scalar.copy(xe[:, 4 * hf:4 * hf + 4].rearrange("p c s -> p (c s)"),
                                   banks[:, 6 + hf, 0:4 * CAP]).then_inc(xe_sb, 1)

            act.wait_ge(table_ready, 1)
            count = act.value_load(n_items[0:1, 0:1], min_val=NE, max_val=MAXI)
            act.wait_ge(xe_ps, 1)
            xe_copies()
            with act.Fori(0, count) as i:
                for g in range(NG):
                    act.wait_ge(mgu_ps, i * NG + (g + 1))
                    if g:
                        act.wait_ge(mhid, i * NG + g)
                    fn(msg, banks[:, g % 2, 0:FS * CAP], ACT.Silu).then_inc(msilu, 1)
                act.wait_ge(mdn_ps, i * NG + NG)
                for hf in range(2):
                    nc.scalar.copy(ynat[0:CAP, 512 * hf:512 * (hf + 1)], banks[0:CAP, 4 + hf, :]).then_inc(yn_sb, 1)
                act.wait_ge(xe_ps, i + 2)
                xe_copies()
            norm(4, so_added, count * NC)
            for w in range(0, 6, 2):
                act.wait_ge(yt_ps, w // 2 + 1)
                rows = P if w < 4 else TS
                nc.scalar.copy(yout[0:rows, w // 2, 0:512], banks[0:rows, w, :]).then_inc(yt_act, 1)

        @block.vector
        def _(dve):
            V = nc.vector
            tt, ts, stt, red = V.tensor_tensor, V.tensor_scalar, V.scalar_tensor_tensor, V.tensor_reduce
            step = Steps(dve, dve_steps)

            def norm(k, v):
                dve.wait_ge(rms_ready, k + 1)
                step(V.reciprocal(rstd[:, :], rms[:, :]))
                step.settle()
                for c in range(NC):
                    stt(hT[:, c], xT[:, c], vecT[:, v, c:c + 1], rstd[:, :], ALU.mult, ALU.mult).then_inc(h_ready, 1)

            V.memset(eps[:, :], EPS).then_inc(eps_ready, 1)
            for c in range(0, NC, 2):
                dve.wait_ge(xt_ps, c + 1)
                V.tensor_copy(xT[:, c], banks[:, c, 0:T]).then_inc(xt_dve, 1)
            dve.wait_ge(vec_ps, 1)
            V.tensor_copy(vecT[:, :, :].rearrange("p v c -> p (v c)"), banks[:, 2, 0:48]).then_inc(vec_sb, 1)
            dve.wait_ge(vec_sb, 1)
            dve.wait_ge(xt_dve, 4)
            dve.wait_ge(xt_act, 4)
            norm(0, V_MIX0)

            dve.wait_ge(h_ready, NC)
            dve.wait_ge(ms_ready, 1)
            dve.wait_ge(consts_in, 16)
            h = hT[:, :, 0:TP]
            for src, dst, shift in ((h, s2, 1), (s2[:, 2:8], s4, 2), (s4[:, 2:6], s8, 4), (s8[:, 2:4], s16, 8)):
                step(tt(dst[:, :, shift:], src[:, :, shift:], src[:, :, 0:TP - shift], ALU.add))
                step(V.tensor_copy(dst[:, :, 0:shift], src[:, :, 0:shift]))
                step.settle()
            dve.wait_ge(st_sb, 2)
            for g, (s, w) in enumerate(zip((s2, s4[:, 0:2], s8[:, 0:2], s16), POOL_WINDOWS)):
                cs = slice(2 * g, 2 * g + 2)
                s = s[:, 0:2]
                step(stt(pl[:, cs, 0:TP], s, 1.0 / w, h[:, cs], ALU.mult, ALU.subtract))
                e = edge_f[:, 0:2 * (w - 1)].rearrange("p (c t) -> p c t", c=2)
                step(tt(e, s[:, :, 0:w - 1], bc(K("inv_cnt")[:, 0:w - 1], 1, 2), ALU.mult))
                step(red(ssum, stT[:, cs, :, 16 - w:], AX, ALU.add))
                step.settle()
                step(tt(pl[:, cs, 0:w - 1], e, h[:, cs, 0:w - 1], ALU.subtract))
                step(tt(ssum, ssum, hT[:, cs, TP:T], ALU.add))
                step.settle()
                stt(pl[:, cs, TP:T], ssum, 1.0 / w, hT[:, cs, TP:T], ALU.mult, ALU.subtract).then_inc(pooled, 1)
                dve.wait_ge(pooled, g + 1)
            for c in range(NC):
                dve.wait_ge(mixed, c + 1)
                stt(xT[:, c], banks[:, c, 0:T], vecT[:, V_POOL, c:c + 1], xT[:, c], ALU.mult, ALU.add
                    ).then_inc(pool_added, 1)
            dve.wait_ge(pool_added, NC)
            dve.wait_ge(po_ps, 2)
            norm(1, V_FFN0)

            def dense_adds(g):
                for d in range(NC):
                    u = NC * g + d
                    dve.wait_ge(down_ps, u + 1)
                    if g:
                        dve.wait_ge(ffn_added, u - NC + 1)
                    tt(xT[:, d], banks[:, 4 + u % 4, 0:T], xT[:, d], ALU.add).then_inc(ffn_added, 1)

            for g in range(NG + 1):
                if g == 1:
                    dve.wait_ge(wkT_ps, 1)
                    V.tensor_copy(wkT[:, :, :, :].rearrange("p a s c -> p (a s c)"), banks[:, 4, 0:128]).then_inc(wkT_sb, 1)
                    tt(wb[:, :, :, :].rearrange("p s k n -> p (s k) n"),
                       bc(wn[:, :, :].rearrange("p s k -> p (s k)"), 2, 4), bc(K("quarter"), 1, 8), ALU.mult).then_inc(wb_ready, 1)
                if g < NG:
                    for s in range(FS):
                        u = FS * g + s
                        dve.wait_ge(silu_done, u + 1)
                        if g >= 2 and s == 0:
                            dve.wait_ge(down_ps, NC * (g - 1))
                        tt(hid[:, g % 2, s], sg[:, u % 2], banks[:, 2 + u % 2, 0:T], ALU.mult).then_inc(hid_done, 1)
                if g:
                    dense_adds(g - 1)
            dve.wait_ge(ffn_added, NC * NG)
            norm(2, V_MIX1)

            def order_queries(q):
                wait_tile(dve, Q_TILE0 + q)
                src = slot_view(Q_SLOT0 + q, "up").rearrange("p c (k g d) -> p c k g d", k=2, g=GQA)
                dst = wq[q].rearrange("p (c g k d) -> p c g k d", c=NC, g=GQA, k=2)
                if q:
                    dve.wait_ge(wq_ready, 2)
                for k2 in range(2):
                    V.tensor_copy(dst[:, :, :, k2, :], src[:, :, k2]).then_inc(wq_ready, 1)

            dve.wait_ge(qz_zero, 3)
            def compress_prompt():
                dve.wait_ge(proj_act, 2)
                dve.wait_ge(proj_dve, 2)
                for s, kind in enumerate((KC_, VC_)):
                    for a in range(2):
                        at = (2 * s + a) * TP
                        step(tt(sc_s[:, at:at + TP].rearrange("p (n c) -> p n c", n=NCMP_P),
                                zkv[:, 2 * kind + a, 0:TP].rearrange("p (n c) -> p n c", n=NCMP_P),
                                bc(wkT[:, a, s, :], 1, NCMP_P), ALU.mult))
                step.settle()
                red(vcp, sc_s[:, 2 * TP:4 * TP].rearrange("p (a n c) -> p a n c", a=2, n=NCMP_P), AX, ALU.add
                    ).then_inc(cp_ready, 1)
                for k2 in range(2):
                    half = slice(HD * k2, HD * (k2 + 1))
                    red(kcz[half, :, k2], sc_s[half, 0:2 * TP].rearrange("p (a n c) -> p a n c", a=2, n=NCMP_P), AX,
                        ALU.add).then_inc(cp_ready, 1)

            order_queries(0)
            for n in range(1, N_PROJ, 2):
                if n == 7:
                    order_queries(1)
                if n == 13:
                    compress_prompt()
                dve.wait_ge(proj_ps, n + 1)
                if n < 12:
                    V.tensor_copy(zkv[:, n], banks[:, n % 4, 0:T]).then_inc(proj_dve, 1)
                else:
                    ts(qT[:, (n - 12) // GQA, (n - 12) % GQA], banks[:, n % 4, 0:T], SCALE, None, ALU.mult
                       ).then_inc(proj_dve, 1)
            dve.wait_ge(vcp_ps, 1)
            V.tensor_copy(vcn_p[0:NCMP_P, :], banks[0:NCMP_P, 7, 0:KVW]).then_inc(vcp_sb, 1)
            for w in range(1, 9, 2):
                dve.wait_ge(nat_ps, w + 1)
                j, quad = divmod(w, 3)
                dst = kvn[:, j, 512 * quad:512 * (quad + 1)] if j < 2 else kvs[0:TS, 512 * quad:512 * (quad + 1)]
                V.tensor_copy(dst, banks[0:(P if j < 2 else TS), 4 + w % 4, :]).then_inc(nat_dve, 1)
            dve.wait_ge(proj_act, 10)
            dve.wait_ge(proj_dve, 10)
            qz0 = 12 * T + 8 * T
            for a in range(2):
                for k2 in range(2):
                    at = qz0 + a * TS * P + (2 * a + k2) * GQA
                    base = arena[HD * k2:HD * (k2 + 1), at:at + GQA]
                    dst = bass.AP(base.tensor, base.offset, [list(base.ap[0]), [P + NH, TS], [1, GQA]])
                    step(V.tensor_copy(dst, qT[HD * k2:HD * (k2 + 1), a, :, TP:T].rearrange("p g b -> p b g")))
                    own = qa[HD * k2:HD * (k2 + 1), a].rearrange("p (b k g) -> p b k g", b=TS, k=NKV)[:, :, 2 * a + k2]
                    last = V.tensor_copy(own, qT[HD * k2:HD * (k2 + 1), a, :, TP:T].rearrange("p g b -> p b g"))
            last.then_inc(qz_ready, 1)
            dve.wait_ge(gate_e, 1)
            step(ts(gn[:, 0:2], gn[:, 0:2], 1.0, None, ALU.add))
            step(ts(gn[0:TS, 2], gn[0:TS, 2], 1.0, None, ALU.add))
            step.settle()
            step(V.reciprocal(gn[:, 0:2], gn[:, 0:2]))
            V.reciprocal(gn[0:TS, 2], gn[0:TS, 2]).then_inc(gates_ready, 1)
            pc3 = pcp_f.rearrange("p (x n) -> p x n", n=NCMP_P)

            def compressed_softmax():
                dve.wait_ge(cs_ps, 1)
                for i in range(2):
                    for a in range(2):
                        pcv, cbv = (v.rearrange("p (i a k g n) -> p i a k g n", i=2, a=2, k=2, g=GQA)[:, i, a]
                                    for v in (pcp_f, K("cmp_bias")))
                        bkv = banks[:, 7, 0:256].rearrange("p (a g i k n) -> p a i k g n", a=2, g=GQA, i=2, k=2)[:, a, i]
                        step(tt(pcv, bkv, cbv, ALU.add))
                step.settle()
                step(red(spread[:, 0:32], pc3, AX, ALU.max))
                step.settle()
                tt(pc3, pc3, bc(spread[:, 0:32], 2, NCMP_P), ALU.subtract).then_inc(cs_in, 1)

            def repeat_values():
                dve.wait_ge(rep_ps, 1)
                for a in range(2):
                    src = bc(banks[:, 2, P * a:P * (a + 1)].rearrange("p (k d) -> p k d", k=2), 1, GQA)
                    mask = bc(K("head_of")[:, 8 * a:8 * (a + 1)].rearrange("p (g k) -> p g k", g=GQA), 3, HD)
                    tt(vcz[:, 4 * a:4 * (a + 1)].rearrange("p g (k d) -> p g k d", k=2), src, mask, ALU.mult
                       ).then_inc(vcz_ready, 1)

            def compressed_weights():
                dve.wait_ge(cs_exp, 1)
                for i in range(2):
                    step(tt(pcp[:, i], pcp[:, i], bc(K("cmp_mask")[:, 8 * i:8 * (i + 1)], 1, NH), ALU.mult))
                step.settle()
                step(red(spread[:, 0:32], pc3, AX, ALU.add))
                step.settle()
                step(ts(spread[:, 0:32], spread[:, 0:32], 1e-30, None, ALU.max))
                step.settle()
                step(V.reciprocal(spread[:, 32:64], spread[:, 0:32]))
                step.settle()
                step(tt(spread[:, 0:32].rearrange("p (i h) -> p i h", i=2),
                        spread[:, 32:64].rearrange("p (i h) -> p i h", i=2), gn[:, 0:2, 0:NH], ALU.mult))
                step.settle()
                tt(pc3, pc3, bc(spread[:, 0:32], 2, NCMP_P), ALU.mult).then_inc(cs_w, 1)

            for n in range(1, UNITS, 2):
                dve.wait_ge(kt_ps, n + 1)
                if n >= 2:
                    dve.wait_ge(sc_done, n - 1)
                V.tensor_copy(KT[:, n % 2], banks[:, 4 + n % 2, :]).then_inc(kt_dve, 1)
                if n == 1:
                    repeat_values()
                if n == 21:
                    compressed_weights()
                if n % 6 == 5:
                    b = n // 6
                    dve.wait_ge(comp_ps, 2 * b + 2)
                    if b >= 2:
                        dve.wait_ge(kc_used, b - 1)
                    for s in range(2):
                        at = s * 128
                        v = banks[:, 6 + b % 2, at:at + 128].rearrange("p (n a k q) -> p a n k q", n=NPAGE, a=2, k=2)
                        dst = (kcT[:, b % 2] if s == 0 else vcT[:, b]).rearrange("p a (n q) -> p a n q", n=NPAGE)
                        for k2 in range(2):
                            half = slice(HD * k2, HD * (k2 + 1))
                            last = V.tensor_copy(dst[half], v[half, :, :, k2, :])
                    last.then_inc(kc_sb, 1)
                if n == 17:
                    compressed_softmax()

            def head(n):
                m, r = divmod(n, 4)
                a, g = divmod(m, GQA)
                k2, i = divmod(r, 2)
                return (2 * a + k2) * GQA + g, i

            def prompt_max(n):
                hd, i = head(n)
                width = P * (i + 1)
                dve.wait_ge(ps_ps, n + 1)
                if n >= 4:
                    dve.wait_ge(pt_ps, n - 3)
                stt(PR[:, n % 4, :, 0:width], bc(K("dist_p")[:, TP - width:TP], 1, 2), float(SLOPES[hd]),
                    banks[:, 4 + n % 2, :].rearrange("p (r t) -> p r t", r=2)[:, :, 0:width], ALU.mult, ALU.add
                    ).then_inc(ps_in, 1)
                dve.wait_ge(ps_in, n + 1)
                red(pst[:, n % 4, NEG_MAX], PR[:, n % 4, :, 0:width], AX, ALU.max, negate=True).then_inc(ps_max, 1)

            dve.wait_ge(sc_done, UNITS)
            dve.wait_ge(kc_used, TS)
            slope = K("slope")
            for hf in range(2):
                step(stt(sc_s[:, 512 * hf:512 * (hf + 1)], K("dist_d")[:, 512 * hf:512 * (hf + 1)], slope,
                         banks[:, hf, :], ALU.mult, ALU.add))
            step(stt(sc_w[:, 0:WIN], K("dist_d")[:, PAST - WIN:], slope, banks[:, 2, :], ALU.mult, ALU.add))
            step.settle()
            step(V.memset(sc_w[:, 0:1], NEG))
            step(tt(pn[:, :, :], banks[:, 3, 0:2 * TS].rearrange("p (r b) -> p r b", r=2), bc(K("is_b"), 1, 2),
                    ALU.mult))
            step.settle()
            step(red(sc_s[:, PAST:PAST + 1], pn[:, 0], AX, ALU.add))
            step(red(sc_w[:, WIN:WIN + 1], pn[:, 1], AX, ALU.add))
            stt(sc_c, K("dist_c"), slope, banks[:, 3, 32:32 + NCMP_D], ALU.mult, ALU.add).then_inc(dec_read, 1)
            dve.wait_ge(dec_read, 1)
            red(sm[:, 0:1], sc_c, AX, ALU.max, negate=True).then_inc(dec_max, 1)
            dve.wait_ge(gd_ps, 1)
            step(tt(gd, banks[:, 6, 64:112].rearrange("p (r h) -> p r h", r=3), bc(K("is_head"), 1, 3), ALU.mult))
            step.settle()
            step(red(gdec, gd, AX, ALU.add))
            dve.wait_ge(dec_exp, 1)
            step(ts(sm[:, 3:4], sm[:, 3:4], 1e-30, None, ALU.max))
            step.settle()
            step(V.reciprocal(sm[:, 6:7], sm[:, 3:4]))
            step.settle()
            step(ts(sc_c, sc_c, sm[:, 6:7], None, ALU.mult))
            step.settle()
            red(sm16[:, 0:NSLC_D], sc_c.rearrange("p (j r) -> p j r", r=SLC // CMP), AX, ALU.add).then_inc(imp_in, 1)
            dve.wait_ge(imp_ps, 1)
            step(tt(sm16[:, 16:32], banks[:, 6, 0:NSLC_D], K("forced"), ALU.add))
            step.settle()
            step(red(sm[:, 7:8], sm16[:, 16:32], AX, ALU.min))
            step.settle()
            step(stt(sm16[:, 32:48], sm16[:, 16:32], sm[:, 7:8], K("order"), ALU.is_equal, ALU.mult))
            step.settle()
            step(red(sm[:, 8:9], sm16[:, 32:48], AX, ALU.max))
            step.settle()
            step(ts(sm16[:, 48:64], sm16[:, 32:48], sm[:, 8:9], NEG, ALU.is_equal, ALU.mult))
            step.settle()
            s3 = sc_s[:, 0:PAST].rearrange("p (j t) -> p j t", t=SLC)
            step(tt(s3, s3, bc(sm16[:, 48:64], 2, SLC), ALU.add))
            step.settle()
            step(red(sm[:, 1:2], sc_s, AX, ALU.max, negate=True))
            red(sm[:, 2:3], sc_w, AX, ALU.max, negate=True).then_inc(dec_max, 1)
            prompt_max(0)
            prompt_max(1)
            dve.wait_ge(dec_exp, 2)
            step(V.reciprocal(sm[:, 9:11], sm[:, 4:6]))
            step.settle()
            step(tt(sm[:, 11:13], sm[:, 9:11], gdec[:, 1:3], ALU.mult))
            step.settle()
            step(ts(sc_c, sc_c, gdec[:, 0:1], None, ALU.mult))
            step(ts(sc_s, sc_s, sm[:, 11:12], None, ALU.mult))
            step(ts(sc_w, sc_w, sm[:, 12:13], None, ALU.mult))
            step.settle()
            step(ts(pn[:, 0, :], K("is_b"), sc_s[:, PAST:PAST + 1], None, ALU.mult))
            ts(pn[:, 1, :], K("is_b"), sc_w[:, WIN:WIN + 1], None, ALU.mult).then_inc(dprob, 1)

            def prompt_weights(n):
                hd, i = head(n)
                width = P * (i + 1)
                o = n % 4
                dve.wait_ge(ps_exp, n + 1)
                step(V.reciprocal(pst[:, o, INV_SUM], pst[:, o, SUM]))
                step.settle()
                step(tt(pst[:, o, WEIGHT], pst[:, o, INV_SUM],
                        gn[:, i, NH:3 * NH].rearrange("p (r h) -> p r h", r=2)[:, :, hd], ALU.mult))
                step.settle()
                tt(PR[:, o, :, 0:width], PR[:, o, :, 0:width], bc(pst[:, o, WEIGHT], 2, width), ALU.mult
                   ).then_inc(pw_ready, 1)

            for n in range(37):
                if 2 <= n < 32:
                    prompt_max(n)
                if 1 <= n < 33:
                    prompt_weights(n - 1)
                if n >= 7 and (n - 7) % 4 == 0:
                    m = (n - 7) // 4
                    dve.wait_ge(pv_done, 4 * m + 4)
                    V.tensor_copy(hT[:, m, 0:TP], banks[:, m % 2, 0:TP]).then_inc(o_sb, 1)
                if n >= 8 and n % 4 == 0:
                    b = n // 4 - 2
                    dve.wait_ge(odt_ps, b + 1)
                    for k2 in range(2):
                        half = slice(HD * k2, HD * (k2 + 1))
                        v = banks[half, 6 + b % 2, KVW:KVW + 48].rearrange("p (a x) -> p a x", a=2)
                        last = V.tensor_copy(hT[half, :, TP + b].rearrange("p (a g) -> p a g", a=2),
                                             v[:, :, GQA * k2:GQA * (k2 + 1)])
                    last.then_inc(od_sb, 1)
            for c in range(NC):
                dve.wait_ge(wo_ps, c + 1)
                tt(xT[:, c], banks[:, 4 + c % 4, 0:T], xT[:, c], ALU.add).then_inc(wo_added, 1)
            dve.wait_ge(wo_added, NC)
            norm(3, V_FFN1)

            R = slice(0, CAP)
            top = one[R]
            dve.wait_ge(stored, 16 * 9)
            dve.wait_ge(lg_ps, 1)
            step(V.tensor_copy(lg[R], banks[R, 6, 0:NTC * NE].rearrange("p (j e) -> p j e", j=NTC)))
            step.settle()
            order3 = bc(K("e_order", CAP), 1, NTC)
            for r, (src, oh) in enumerate(((lg, oh1), (l2, oh2))):
                m = top[:, 3 * r:3 * r + 3]
                step(red(m, src[R], AX, ALU.max))
                step.settle()
                step(tt(eq[R], src[R], bc(m, 2, NE), ALU.is_equal))
                step.settle()
                step(tt(eq[R], eq[R], order3, ALU.mult))
                step.settle()
                step(red(top[:, 9:12], eq[R], AX, ALU.max))
                step.settle()
                step(tt(oh[R], eq[R], bc(top[:, 9:12], 2, NE), ALU.is_equal))
                step.settle()
                if r == 0:
                    step(stt(l2[R], oh1[R], NEG, lg[R], ALU.mult, ALU.add))
                    step.settle()
            step(tt(sel[R], oh1[R], oh2[R], ALU.add))
            step.settle()
            tt(top[:, 6:9], top[:, 3:6], top[:, 0:3], ALU.subtract).then_inc(top_gap, 1)
            V.tensor_copy(sel[R], sel[R]).then_inc(sel_ready, 1)
            for w in range(1, 6, 2):
                dve.wait_ge(xn_ps, w + 1)
                V.tensor_copy(xn[0:CAP, w // 2, 512:1024], banks[0:CAP, w, :]).then_inc(xn_dve, 1)
            dve.wait_ge(top_exp, 1)
            step(ts(top[:, 12:15], top[:, 6:9], 1.0, None, ALU.add))
            step.settle()
            step(V.reciprocal(top[:, 15:18], top[:, 12:15]))
            step.settle()
            step(tt(top[:, 18:21], top[:, 15:18], top[:, 6:9], ALU.mult))
            step(tt(oh1[R], oh1[R], bc(top[:, 15:18], 2, NE), ALU.mult))
            step.settle()
            step(tt(oh2[R], oh2[R], bc(top[:, 18:21], 2, NE), ALU.mult))
            step.settle()
            for r in range(3):
                step(tt(gx[R, :, r], oh1[R], oh2[R], ALU.add))
            dve.wait_ge(pos_ps, 1)
            step(stt(l2[R], banks[R, 6, 32:32 + NTC * NE].rearrange("p (j e) -> p j e", j=NTC), 1.0, sel[R], ALU.add,
                     ALU.mult))
            step.settle()
            for r in range(3):
                step(ts(posx[R, :, r], l2[R], -1.0 - r * CAP, None, ALU.add))
            step.settle()
            for r in range(2):
                step(V.tensor_copy(ovr[0:1, NE * r:NE * (r + 1)], banks[0:1, 6, 64:64 + NE]))
            step(V.tensor_copy(items_f[0:1, 0:MAXI + 1], K("items0", 1)))
            step.settle()
            step(tt(ovr[0:1, 16:32], ovr[0:1, 0:16], K("over_min", 1), ALU.is_gt))
            step.settle()
            step(tt(ovr[0:1, 32:48], ovr[0:1, 16:32], K("over_code", 1), ALU.mult))
            step(red(ovr[0:1, 48:49], ovr[0:1, 16:32], AX, ALU.add))
            step.settle()
            step(V.max(items_f[0:1, NE:2 * NE], ovr[0:1, 32:48]))
            step(ts(ovr[0:1, 49:50], ovr[0:1, 48:49], float(NE), None, ALU.add))
            step.settle()
            V.tensor_copy(items[0:1, :], items_f[0:1, 0:MAXI + 1]).then_inc(so_added, NC)
            dve.wait_ge(so_added, NC)
            V.tensor_copy(n_items[0:1, :], ovr[0:1, 49:50]).then_inc(table_ready, 1)
            dve.wait_ge(table_ready, 1)
            step.settle()
            count = dve.value_load(n_items[0:1, 0:1], min_val=NE, max_val=MAXI)

            def code_of(i):
                return dve.value_load(items[0:1, i:i + 1] if isinstance(i, int) else items[0:1, bass.ds(i, 1)],
                                      min_val=0, max_val=3 * NE - 1)

            def places(code):
                for j in range(NTC):
                    last = ts(Pm[R, j], K("iota_s", CAP), posc[R, j, bass.ds(code, 1)], None, ALU.is_equal)
                last.then_inc(P_ready, 1)

            places(code_of(0))
            with dve.Fori(0, count) as i:
                for g in range(NG):
                    dve.wait_ge(msilu, i * NG + (g + 1))
                    if g >= 2:
                        dve.wait_ge(mdn_ps, i * NG + (g - 1))
                    tt(mh[:, g % 2].rearrange("p f s -> p (f s)"), msg, banks[:, 2 + g % 2, 0:FS * CAP], ALU.mult
                       ).then_inc(mhid, 1)
                    if g == 0:
                        code = code_of(i)
                        for j in range(NTC):
                            last = ts(Gm[R, j], K("iota_s", CAP), posc[R, j, bass.ds(code, 1)],
                                      gxc[R, j, bass.ds(code, 1)], ALU.is_equal, ALU.mult)
                        last.then_inc(G_ready, 1)
                    if g == 1:
                        places(code_of(i + 1))
                dve.wait_ge(gt_ps, i + 1)
                V.tensor_copy(GT[R], banks[R, 1, 0:T]).then_inc(gt_sb, 1)
                for c in range(NC):
                    dve.wait_ge(so_ps, i * NC + (c + 1))
                    tt(xT[:, c], banks[:, (6, 7, 1, 3)[c % 4], 0:T], xT[:, c], ALU.add).then_inc(so_added, 1)
            dve.wait_ge(so_added, count * NC + NC)
            norm(4, V_FINAL)
            for w in range(1, 6, 2):
                dve.wait_ge(yt_ps, 3 + w // 2 + 1)
                rows = P if w < 4 else TS
                V.tensor_copy(yout[0:rows, w // 2, 512:1024], banks[0:rows, w, :]).then_inc(yt_dve, 1)


INPUTS = ["x_prompt", "x_sample", "state_pool", "cache_kv", "state_win", "page_table", "norm_mix", "w_pool",
          "pool_scale", "w_nsa_in", "w_cmp_k", "w_cmp_v", "w_nsa_out", "norm_ffn", "w_ffn_gate", "w_ffn_up",
          "w_ffn_down", "w_router", "w_moe_gate", "w_moe_up", "w_moe_down", "norm_final"]
OUTPUTS = [(1, TP, D), (TS, 1, D), (1, 1, POOL_BUF, D), (1, TS, POOL_BUF, D), (1, 1, TP, 4, NKV, HD),
           (1, TS, 1, 4, NKV, HD), (1, 1, TP, 2, NKV, HD), (1, TS, WIN, 2, NKV, HD)]


def kernel(**inputs):
    import concourse.bacc as bacc
    from concourse.bass_utils import run_bass_kernel_spmd as run

    nc = bacc.Bacc("TRN2", target_bir_lowering=False, num_devices=1)
    arrays, args = {}, []
    for name in INPUTS:
        a = np.ascontiguousarray(inputs[name])
        arrays["in_" + name] = a
        args.append(nc.dram_tensor("in_" + name, a.shape, mybir.dt.from_np(a.dtype), kind="ExternalInput").ap())
    table = np.concatenate(list(constants().values()), axis=1)
    arrays["in_consts"] = table
    args.append(nc.dram_tensor("in_consts", table.shape, F32, kind="ExternalInput").ap())
    for i, shape in enumerate(OUTPUTS):
        args.append(nc.dram_tensor(f"out_{i}", shape, F32, kind="ExternalOutput").ap())
    build(nc, *args)
    r = run(nc, [arrays], core_ids=[0])
    return tuple(r.results[0][f"out_{i}"] for i in range(len(OUTPUTS)))
```
